# Optimizing a Trainium2 kernel written in Bass

```python
import jax, jax.numpy as jnp
from jax import lax
import numpy as np

D_MODEL = 1024
BATCH = 1
SEQ = 1024
DEPTH = 1
DEC_BATCH = 8
DEC_SEQ = 8
PAST_LEN = 8192
PAGE_SIZE = 128

D_MIX = D_MODEL
A_WIDTH = D_MIX // 2
B_WIDTH = D_MIX - A_WIDTH
A_HEADS = 4
A_HEAD_DIM = A_WIDTH // A_HEADS
CHUNK = 128
B_GROUPS = 4
B_GROUP_DIM = B_WIDTH // B_GROUPS
POOL_WINDOWS = (2, 4, 8, 16)
POOL_STATE = max(POOL_WINDOWS) - 1
N_EXPERT_GROUPS = 4
EXPERTS_PER_GROUP = 8
N_EXPERTS = N_EXPERT_GROUPS * EXPERTS_PER_GROUP
TOP_K = 2
D_EXPERT = D_MODEL // 2
MOE_BLOCK = 128
EPS = 1e-6

kernel_name = "hymba_gmlp_pool_hmoe_step"

def rmsnorm(x, g):
    xf = x.astype(jnp.float32)
    r = lax.rsqrt(jnp.mean(xf * xf, axis=-1, keepdims=True) + EPS)
    return (xf * r).astype(x.dtype) * g

def layernorm(x, g, b):
    xf = x.astype(jnp.float32)
    mu = jnp.mean(xf, axis=-1, keepdims=True)
    var = jnp.mean(jnp.square(xf - mu), axis=-1, keepdims=True)
    return ((xf - mu) * lax.rsqrt(var + EPS)).astype(x.dtype) * g + b

def chunk_spatial_gate(u, v, a_ws, a_bs, chunk_len):
    bsz, L, _ = v.shape
    nc = L // chunk_len
    vh = v.reshape(bsz, nc, chunk_len, A_HEADS, A_HEAD_DIM)
    uh = u.reshape(bsz, nc, chunk_len, A_HEADS, A_HEAD_DIM)
    mask = jnp.tril(jnp.ones((chunk_len, chunk_len), dtype=bool))
    ws = jnp.where(mask, a_ws[:, :chunk_len, :chunk_len], jnp.zeros((), a_ws.dtype))
    z = jnp.einsum('hts,bcshd->bcthd', ws, vh) + a_bs[:, :chunk_len].T[None, None, :, :, None]
    return (uh * z).reshape(bsz, L, A_WIDTH)

def multiscale_pool(p, prefix, pos, b_w, b_scale):
    bsz, L, _ = p.shape
    ext = jnp.concatenate([prefix, p], axis=1).astype(jnp.float32)
    c = jnp.cumsum(ext, axis=1)
    c = jnp.concatenate([jnp.zeros((bsz, 1, B_WIDTH), jnp.float32), c], axis=1)
    outs = []
    for g, w in enumerate(POOL_WINDOWS):
        lo, hi = g * B_GROUP_DIM, (g + 1) * B_GROUP_DIM
        s = c[:, POOL_STATE + 1:, lo:hi] - c[:, POOL_STATE + 1 - w:POOL_STATE + 1 - w + L, lo:hi]
        cnt = jnp.minimum(pos + 1, w).astype(jnp.float32)[None, :, None]
        outs.append(s / cnt)
    pooled = jnp.concatenate(outs, axis=-1).astype(p.dtype) - p
    h = jnp.einsum('blgc,gcd->blgd', pooled.reshape(bsz, L, B_GROUPS, B_GROUP_DIM), b_w)
    return h.reshape(bsz, L, B_WIDTH) * b_scale

def hier_route(x2d, r1_w, r1_b, r2_w, r2_b):
    xf = x2d.astype(jnp.float32)
    l1 = xf @ r1_w.astype(jnp.float32) + r1_b.astype(jnp.float32)
    p1 = jax.nn.softmax(l1, axis=-1)
    grp = jnp.argmax(l1, axis=-1)
    pg = jnp.take_along_axis(p1, grp[:, None], axis=1)[:, 0]
    l2 = jnp.einsum('td,gde->tge', xf, r2_w.astype(jnp.float32)) + r2_b.astype(jnp.float32)
    l2g = jnp.take_along_axis(l2, grp[:, None, None], axis=1)[:, 0]
    top_v, top_i = lax.top_k(l2g, TOP_K)
    gates = jax.nn.softmax(top_v, axis=-1) * pg[:, None]
    eidx = grp[:, None] * EXPERTS_PER_GROUP + top_i
    return eidx, gates

def moe_ffn(x2d, eidx, gates, w1, w3, w2):
    T, D = x2d.shape
    A = T * TOP_K
    flat_e = eidx.reshape(-1)
    order = jnp.argsort(flat_e)
    sorted_e = flat_e[order]
    tok = order // TOP_K
    counts = jnp.bincount(flat_e, length=N_EXPERTS)
    padded = (counts + MOE_BLOCK - 1) // MOE_BLOCK * MOE_BLOCK
    pad_end = jnp.cumsum(padded)
    pad_start = pad_end - padded
    seg_start = jnp.cumsum(counts) - counts
    rank = jnp.arange(A, dtype=jnp.int32) - seg_start[sorted_e]
    dest = pad_start[sorted_e] + rank
    nb = (A + N_EXPERTS * (MOE_BLOCK - 1) + MOE_BLOCK - 1) // MOE_BLOCK
    xs = jnp.zeros((nb * MOE_BLOCK, D), x2d.dtype).at[dest].set(x2d[tok])
    block_e = jnp.minimum(jnp.searchsorted(pad_end, jnp.arange(nb) * MOE_BLOCK, side='right'),
                          N_EXPERTS - 1)

    def expert_block(args):
        xb, e = args
        h = jax.nn.silu(xb @ w1[e]) * (xb @ w3[e])
        return h @ w2[e]

    out = lax.map(expert_block, (xs.reshape(nb, MOE_BLOCK, D), block_e)).reshape(nb * MOE_BLOCK, D)
    g_sorted = gates.reshape(-1)[order].astype(x2d.dtype)
    return jax.ops.segment_sum(out[dest] * g_sorted[:, None], tok, num_segments=T)

def layer(x, pool_prefix, pos, chunk_len, norm1_g, w_in, a_norm_g, a_norm_b, a_ws, a_bs,
          b_w, b_scale, w_out, norm2_g, r1_w, r1_b, r2_w, r2_b, exp_w1, exp_w3, exp_w2):
    bsz, L, D = x.shape
    h = rmsnorm(x, norm1_g)
    proj = h @ w_in
    uv = jax.nn.gelu(proj[..., :2 * A_WIDTH], approximate=False)
    u = uv[..., :A_WIDTH]
    v = layernorm(uv[..., A_WIDTH:], a_norm_g, a_norm_b)
    p = proj[..., 2 * A_WIDTH:]
    ya = chunk_spatial_gate(u, v, a_ws, a_bs, chunk_len)
    yb = multiscale_pool(p, pool_prefix, pos, b_w, b_scale)
    x = x + jnp.concatenate([ya, yb], axis=-1) @ w_out
    h2 = rmsnorm(x, norm2_g).reshape(bsz * L, D)
    eidx, gates = hier_route(h2, r1_w, r1_b, r2_w, r2_b)
    x = x + moe_ffn(h2, eidx, gates, exp_w1, exp_w3, exp_w2).reshape(bsz, L, D)
    return x, p, v

def setup_inputs(seed: int = 0) -> dict:
    key = jax.random.key(seed)
    ks = jax.random.split(key, 24)
    f = jnp.float32
    nrm = lambda k, shape, s: jax.random.normal(k, shape, f) * s
    return {
        "x_prompt": nrm(ks[0], (BATCH, SEQ, D_MODEL), 1.0),
        "x_sample": nrm(ks[1], (DEC_BATCH, DEC_SEQ, D_MODEL), 1.0),
        "state_pool": nrm(ks[2], (DEPTH, DEC_BATCH, POOL_STATE, B_WIDTH), 1.0),
        "norm1_g": 1.0 + nrm(ks[3], (DEPTH, D_MODEL), 0.02),
        "w_in": nrm(ks[4], (DEPTH, D_MODEL, 2 * A_WIDTH + B_WIDTH), D_MODEL ** -0.5),
        "a_norm_g": 1.0 + nrm(ks[5], (DEPTH, A_WIDTH), 0.02),
        "a_norm_b": nrm(ks[6], (DEPTH, A_WIDTH), 0.02),
        "a_ws": nrm(ks[7], (DEPTH, A_HEADS, CHUNK, CHUNK), 0.5 * CHUNK ** -0.5),
        "a_bs": 1.0 + nrm(ks[8], (DEPTH, A_HEADS, CHUNK), 0.1),
        "b_w": nrm(ks[9], (DEPTH, B_GROUPS, B_GROUP_DIM, B_GROUP_DIM), B_GROUP_DIM ** -0.5),
        "b_scale": 1.0 + nrm(ks[10], (DEPTH, B_WIDTH), 0.1),
        "w_out": nrm(ks[11], (DEPTH, D_MIX, D_MODEL), D_MIX ** -0.5),
        "norm2_g": 1.0 + nrm(ks[12], (DEPTH, D_MODEL), 0.02),
        "r1_w": nrm(ks[13], (DEPTH, D_MODEL, N_EXPERT_GROUPS), D_MODEL ** -0.5),
        "r1_b": nrm(ks[14], (DEPTH, N_EXPERT_GROUPS), 0.01),
        "r2_w": nrm(ks[15], (DEPTH, N_EXPERT_GROUPS, D_MODEL, EXPERTS_PER_GROUP), D_MODEL ** -0.5),
        "r2_b": nrm(ks[16], (DEPTH, N_EXPERT_GROUPS, EXPERTS_PER_GROUP), 0.01),
        "exp_w1": nrm(ks[17], (DEPTH, N_EXPERTS, D_MODEL, D_EXPERT), D_MODEL ** -0.5),
        "exp_w3": nrm(ks[18], (DEPTH, N_EXPERTS, D_MODEL, D_EXPERT), D_MODEL ** -0.5),
        "exp_w2": nrm(ks[19], (DEPTH, N_EXPERTS, D_EXPERT, D_MODEL), D_EXPERT ** -0.5),
        "normf_g": 1.0 + nrm(ks[20], (D_MODEL,), 0.02),
    }

def reference(x_prompt, x_sample, state_pool, norm1_g, w_in, a_norm_g, a_norm_b, a_ws, a_bs,
              b_w, b_scale, w_out, norm2_g, r1_w, r1_b, r2_w, r2_b, exp_w1, exp_w3, exp_w2, normf_g):
    seq = x_prompt.shape[1]
    dec_seq = x_sample.shape[1]
    pos_prompt = jnp.arange(seq, dtype=jnp.int32)
    pos_sample = PAST_LEN + jnp.arange(dec_seq, dtype=jnp.int32)
    zero_prefix = jnp.zeros((x_prompt.shape[0], POOL_STATE, B_WIDTH), x_prompt.dtype)
    xp, xs = x_prompt, x_sample
    pool_p, pool_s, v_s = [], [], []
    for l in range(DEPTH):
        prm = (norm1_g[l], w_in[l], a_norm_g[l], a_norm_b[l], a_ws[l], a_bs[l], b_w[l], b_scale[l],
               w_out[l], norm2_g[l], r1_w[l], r1_b[l], r2_w[l], r2_b[l], exp_w1[l], exp_w3[l], exp_w2[l])
        xp, p_p, _ = layer(xp, zero_prefix, pos_prompt, CHUNK, *prm)
        xs, p_s, v_new = layer(xs, state_pool[l], pos_sample, dec_seq, *prm)
        pool_p.append(p_p[:, -POOL_STATE:])
        pool_s.append(jnp.concatenate([state_pool[l], p_s], axis=1)[:, -POOL_STATE:])
        v_s.append(v_new)
    y_prompt = rmsnorm(xp, normf_g)
    y_sample = rmsnorm(xs, normf_g)
    pool_state_prompt = jnp.stack(pool_p, axis=0)
    pool_state_sample = jnp.stack(pool_s, axis=0)
    chunk_v_sample = jnp.stack(v_s, axis=0)
    return (y_prompt, y_sample, pool_state_prompt, pool_state_sample, chunk_v_sample)


_drawn_inputs = setup_inputs


def setup_inputs(seed=0):
    import zlib

    import numpy as np

    out = dict(_drawn_inputs(seed))
    spreads = {}
    factors = {'a_norm_g': 21.225,
     'a_norm_b': 21.122,
     'r1_b': 10.583,
     'normf_g': 25.609,
     'r2_b': 7.808,
     'norm2_g': 2.796}
    for name, (base, spread) in spreads.items():
        noise = np.random.default_rng([zlib.crc32(name.encode()), seed]).standard_normal(out[name].shape)
        drawn = base * np.exp(spread * noise) if base else spread * noise
        out[name] = __import__('jax').numpy.asarray(drawn.astype(out[name].dtype))
    for name, factor in factors.items():
        out[name] = (out[name] * factor).astype(out[name].dtype)
    return out
```

```python
from contextlib import ExitStack

import concourse.bass as bass
from concourse import mybir

P = 128
D = 1024
SEQ = 1024
NS = 64
DEC, DSEQ = 8, 8
T = SEQ + NS
NT = SEQ // P + 1
KD = D // P
AW = 512
HEADS = GROUPS = 4
STATE = 15
WINDOWS = (2, 4, 8, 16)
TAIL = 32
NG, NE, EPG = 4, 32, 8
NR = NG + NE
FE = 512
KF = FE // P
MINB = 18
MAXB = 48
TB = MAXB + 2
THRESH = 9
EPS = 1e-6
BIG = 1.0e30
RSTEPS = 11
NOWHERE = 1 << 14

F32 = mybir.dt.float32
I32 = mybir.dt.int32
ALU = mybir.AluOpType
ACT = mybir.ActivationFunctionType
AX = mybir.AxisListType.X


def reached(eng, sem, n):
    if not isinstance(n, int) or n > 0:
        eng.wait_ge(sem, n)


def build(nc, x_prompt, x_sample, state_pool, norm1_g, w_in, a_norm_g, a_norm_b, ws_sht, bs_th,
          b_w, bsc_dg, w_out, norm2_g, r_w, r_b, exp_w1, exp_w3, exp_w2, normf_g,
          c_ident, c_band, c_band_first, c_band_prev, c_band_s, c_band_state, c_tri, c_row, c_ids,
          y_prompt, y_sample, pool_p, pool_s, v_s):
    ctx = ExitStack()
    with ctx:
        def sb(name, shape, dt=F32):
            return ctx.enter_context(nc.sbuf_tensor(name, shape, dt))

        def sem(name):
            return ctx.enter_context(nc.semaphore(name))

        h2_rows = nc.dram_tensor("h2_rows", [T, D], F32, kind="Internal").ap()
        pair_rows = nc.dram_tensor("pair_rows", [2 * T, D], F32, kind="Internal").ap()
        slot_table = nc.dram_tensor("slot_table", [TB * P, 4], I32, kind="Internal").ap()

        xres = sb("xres", [P, NT, D])
        big = sb("big", [P, 2, 3 * KD * FE])
        flat = big[:, :, :].rearrange("p a n -> p (a n)")
        win = flat[:, 0:KD * 3 * AW].rearrange("p (k n) -> p k n", k=KD)
        wout = flat[:, KD * 3 * AW:KD * (3 * AW + D)].rearrange("p (k n) -> p k n", k=KD)
        ew1 = [big[:, s, 0:4096].rearrange("p (k n) -> p k n", k=KD) for s in range(2)]
        ew3 = [big[:, s, 4096:8192].rearrange("p (k n) -> p k n", k=KD) for s in range(2)]
        ew2 = [big[:, s, 8192:12288].rearrange("p (k n) -> p k n", k=KF) for s in range(2)]

        ident = sb("ident", [P, P])
        band = sb("band", [P, GROUPS, P])
        band_first = sb("band_first", [P, GROUPS, P])
        band_prev = sb("band_prev", [P, GROUPS, P])
        band_s = sb("band_s", [P, GROUPS, NS])
        band_state = sb("band_state", [P, GROUPS, NS])
        state = sb("state", [P, AW])
        tri = sb("tri", [P, P])
        ones = sb("ones", [P, P])
        wst = sb("wst", [P, HEADS, P])
        wst_s = sb("wst_s", [P, HEADS, NS])
        bst = sb("bst", [P, HEADS])
        bst_s = sb("bst_s", [P, HEADS])
        g1t = sb("g1t", [P, KD])
        g2t = sb("g2t", [P, KD])
        ag = sb("ag", [P, AW])
        ab = sb("ab", [P, AW])
        gf = sb("gf", [P, D])
        bw = sb("bw", [P, GROUPS, P])
        bsc = sb("bsc", [P, GROUPS])
        rw = sb("rw", [P, KD, NR])
        rb = sb("rb", [P, NR])
        crow = sb("crow", [P, NG + NE + MAXB + THRESH])
        ids = sb("ids", [P, NT, 2, 4], I32)

        xn = sb("xn", [P, D])
        hT = sb("hT", [P, KD, P])
        u = sb("u", [P, AW])
        vg = sb("vg", [P, AW])
        v = sb("v", [P, AW])
        p = sb("p", [P, AW])
        ptail = sb("ptail", [P, AW])
        poolT = sb("poolT", [P, GROUPS, P])
        ya = sb("ya", [P, AW])
        yT = sb("yT", [P, KD, P])
        xn2 = sb("xn2", [P, D])
        h2T = sb("h2T", [P, KD, P])
        junk = sb("junk", [P, D])
        ss1 = sb("ss1", [P, 4])
        ss2 = sb("ss2", [P, 4])
        lnst = sb("lnst", [P, 16])
        logits = sb("logits", [P, NT, NR])

        xg = [sb(f"xg{s}", [P, D]) for s in range(2)]
        slot = [sb(f"slot{s}", [P, 4], I32) for s in range(2)]
        xT = hT
        s1 = u
        hh = v
        hhT = poolT
        ys = [xn, xn2]
        ypair = [flat[:, 0:2 * D], flat[:, 3 * KD * FE:3 * KD * FE + 2 * D]]

        ra = sb("ra", [P, NT, 2 * NG])
        rd = sb("rd", [P, NT, NG])
        rv = sb("rv", [P, 8, NT])
        rm = junk[:, 0:NT * NE].rearrange("p (j e) -> p j e", e=NE)
        oh1 = vg[:, 0:NT * NE].rearrange("p (j e) -> p j e", e=NE)
        oh2 = ya[:, 0:NT * NE].rearrange("p (j e) -> p j e", e=NE)
        mk = band_first[:, :, :].rearrange("p g n -> p (g n)")[:, 0:NT * NE].rearrange("p (j e) -> p j e", e=NE)
        base = band_prev[:, :, :].rearrange("p g n -> p (g n)")[:, 0:(NT + 1) * NE].rearrange("p (j e) -> p j e", e=NE)
        blk = sb("blk", [P, 3, NE])
        cmp = flat[:, 0:MAXB * NE]
        planf = sb("planf", [1, MAXB + 1])
        plan = sb("plan", [1, MAXB + 1], I32)
        dest = sb("dest", [P, NT, 2], mybir.dt.uint32)

        ps = ctx.enter_context(nc.psum_tensor("ps", [P, 8, 512], F32))
        wide = ps[:, 0:2, :].rearrange("p a (k n) -> p (a k) n", n=P)

        in_first = sem("in_first")
        in_small = sem("in_small")
        in_x0 = sem("in_x0")
        in_x = sem("in_x")
        in_win = [sem(f"in_win{q}") for q in range(4)]
        in_wout = sem("in_wout")
        in_filler = sem("in_filler")
        state_moved = sem("state_moved")
        sq1 = sem("sq1")
        rs1 = sem("rs1")
        rs1_step = sem("rs1_step")
        xn_ready = sem("xn_ready")
        xT_done = sem("xT_done")
        hT_ready = sem("hT_ready")
        proj_v = sem("proj_v")
        proj_u = sem("proj_u")
        proj_p = sem("proj_p")
        v_gelu = sem("v_gelu")
        u_gelu = sem("u_gelu")
        p_copied = sem("p_copied")
        ln_step = sem("ln_step")
        ln_rs_step = sem("ln_rs_step")
        ln_rs = sem("ln_rs")
        v_ready = sem("v_ready")
        z_done = sem("z_done")
        pooled = sem("pooled")
        ya_ready = sem("ya_ready")
        poolT_ready = sem("poolT_ready")
        ptail_ready = sem("ptail_ready")
        yb_done = sem("yb_done")
        yaT_done = sem("yaT_done")
        yaT_ready = sem("yaT_ready")
        ybT_ready = sem("ybT_ready")
        out_a = sem("out_a")
        out_b = sem("out_b")
        x2a_ready = sem("x2a_ready")
        x2_ready = sem("x2_ready")
        sq2 = sem("sq2")
        rs2 = sem("rs2")
        rs2_step = sem("rs2_step")
        x2n_ready = sem("x2n_ready")
        h2_stored = sem("h2_stored")
        x2T_done = sem("x2T_done")
        h2T_ready = sem("h2T_ready")
        logit_done = sem("logit_done")
        logits_ready = sem("logits_ready")
        zeroed = sem("zeroed")
        filled = sem("filled")
        wst_masked = sem("wst_masked")
        p7_stored = sem("p7_stored")
        outs = sem("outs")
        rt = sem("rt")
        rt_exp = sem("rt_exp")
        rt_rank = sem("rt_rank")
        table_stored = sem("table_stored")
        w1_in = [sem(f"w1_in{s}") for s in range(2)]
        w3_in = [sem(f"w3_in{s}") for s in range(2)]
        w2_in = [sem(f"w2_in{s}") for s in range(2)]
        slot_in = [sem(f"slot_in{s}") for s in range(2)]
        rows_in = [sem(f"rows_in{s}") for s in range(2)]
        rows_out = [sem(f"rows_out{s}") for s in range(2)]
        xgT_done = sem("xgT_done")
        xgT_ready = sem("xgT_ready")
        up1 = sem("up1")
        up3 = sem("up3")
        silu_done = sem("silu_done")
        hh_ready = sem("hh_ready")
        hhT_done = sem("hhT_done")
        hhT_ready = sem("hhT_ready")
        down = sem("down")
        y_ready = sem("y_ready")
        pair_in = [sem(f"pair_in{q}") for q in range(2)]
        y_stored = [sem(f"y_stored{q}") for q in range(2)]
        pair_sum = sem("pair_sum")
        x3_ready = sem("x3_ready")
        sq3 = sem("sq3")
        rs3 = sem("rs3")
        rs3_step = sem("rs3_step")
        y_out = sem("y_out")

        LAST = NT - 1
        small = []
        rt_at = {"d1": 2, "d2": 37, "mask": 39, "plan": 67, "table": 75}

        def m_of(kind):
            return NS if kind == "sample" else P

        def drain(step):
            step(LAST - 1, "mid", "mid", "sample")
            step(LAST, "sample", "mid", None)
            step(LAST + 1, None, "sample", None)

        block = ctx.enter_context(nc.Block())

        @block.sync
        def _(sp):
            xp = x_prompt[0]

            def load(dst, src):
                small.append(1)
                sp.dma_start(dst, src).then_inc(in_small, 16)

            sp.dma_start(xres[:, 0, :], xp[0:P, :]).then_inc(in_x0, 16)
            sp.dma_start(ident[:, :], c_ident).then_inc(in_first, 16)
            sp.dma_start(g1t[:, :], norm1_g[0].rearrange("(p k) -> p k", k=KD)).then_inc(in_first, 16)
            wv = w_in[0].rearrange("(p k) n -> p k n", k=KD)
            for q in range(4):
                sp.dma_start(win[:, 2 * q:2 * q + 2, :], wv[:, 2 * q:2 * q + 2, :]).then_inc(in_win[q], 16)
            load(ag[:, :], a_norm_g[0].partition_broadcast(P))
            load(ab[:, :], a_norm_b[0].partition_broadcast(P))
            load(wst[:, :, :], ws_sht)
            load(bst[:, :], bs_th)
            load(band_first[:, :, :], c_band_first)
            load(band[:, :, :], c_band)
            load(band_prev[:, :, :], c_band_prev)
            load(bw[:, :, :], b_w[0].rearrange("g c d -> c g d"))
            load(bsc[:, :], bsc_dg)
            load(g2t[:, :], norm2_g[0].rearrange("(p k) -> p k", k=KD))
            load(rw[:, :, :], r_w.rearrange("(p k) n -> p k n", k=KD))
            load(rb[:, :], r_b.partition_broadcast(P))
            load(band_s[0:NS, :, :], c_band_s)
            load(band_state[0:DEC * STATE, :, :], c_band_state)
            load(state[0:DEC * STATE, :], state_pool[0].rearrange("b s c -> (b s) c"))
            load(tri[:, :], c_tri)
            load(crow[:, :], c_row.partition_broadcast(P))
            load(ids[:, :, :, :], c_ids)
            load(gf[:, :], normf_g.partition_broadcast(P))
            sp.wait_ge(zeroed, 1)
            for b in range(DEC):
                r = slice(b * DSEQ, (b + 1) * DSEQ)
                load(wst_s[r, :, r], ws_sht[0:DSEQ, :, 0:DSEQ])
                load(bst_s[r, :], bs_th[0:DSEQ, :])
            sp.dma_start(xres[:, 1:NT - 1, :],
                         xp[P:SEQ, :].rearrange("(j p) d -> p j d", p=P)).then_inc(in_x, 16)
            sp.dma_start(xres[0:NS, NT - 1, :], x_sample.rearrange("b s d -> (b s) d")).then_inc(in_x, 16)
            sp.dma_start(wout[:, 0:HEADS, :],
                         w_out[0, 0:AW, :].rearrange("(p k) n -> p k n", k=HEADS)).then_inc(in_wout, 16)
            sp.dma_start(wout[:, HEADS:KD, :],
                         w_out[0, AW:D, :].rearrange("(g d) n -> d g n", g=GROUPS)).then_inc(in_wout, 16)
            sp.dma_start(pool_s[0, :, 0:STATE - DSEQ, :],
                         state_pool[0, :, DSEQ:STATE, :]).then_inc(state_moved, 16)
            sp.wait_ge(filled, 1)
            sp.dma_start(slot_table.rearrange("(p q) c -> p (q c)", p=P),
                         xg[0][:, 0:TB * 4].bitcast(I32)).then_inc(in_filler, 16)

            def store_h2(i, m=P):
                reached(sp, x2n_ready, i + 1)
                sp.dma_start(h2_rows[bass.ts(i, P), :] if m == P else h2_rows[SEQ:T, :],
                             xn2[0:m, :]).then_inc(h2_stored, 16)

            with sp.Fori(0, LAST - 1) as i:
                store_h2(i)
            sp.wait_ge(p_copied, LAST)
            sp.dma_start(pool_p[0, 0], p[P - STATE:P, :]).then_inc(p7_stored, 16)
            store_h2(LAST - 1)
            sp.wait_ge(p_copied, NT)
            for b in range(DEC):
                sp.dma_start(pool_s[0, b, STATE - DSEQ:STATE, :],
                             p[b * DSEQ:(b + 1) * DSEQ, :]).then_inc(outs, 16)
            sp.wait_ge(v_ready, NT)
            sp.dma_start(v_s[0].rearrange("b s c -> (b s) c"), v[0:NS, :]).then_inc(outs, 16)
            store_h2(LAST, NS)
            sp.wait_ge(outs, 16 * (DEC + 1))

            def load_expert(b, s):
                e = sp.value_load(plan[0:1, bass.ds(b, 1)], min_val=0, max_val=NE - 1)
                sp.dma_start(ew1[s], exp_w1[0, e].rearrange("(p k) n -> p k n", k=KD)).then_inc(w1_in[s], 16)
                sp.dma_start(ew3[s], exp_w3[0, e].rearrange("(p k) n -> p k n", k=KD)).then_inc(w3_in[s], 16)
                sp.dma_start(ew2[s], exp_w2[0, e].rearrange("(p k) n -> p k n", k=KF)).then_inc(w2_in[s], 16)

            sp.wait_ge(rt, rt_at["plan"])
            np2 = sp.value_load(plan[0:1, MAXB:MAXB + 1], min_val=MINB // 2, max_val=MAXB // 2)
            sp.wait_ge(out_b, NT)
            load_expert(0, 0)
            load_expert(1, 1)
            with sp.Fori(1, np2) as h:
                for s in range(2):
                    sp.wait_ge(down, 2 * h + s - 1)
                    load_expert(2 * h + s, s)

            def load_pairs(turn, q, m=P):
                src = pair_rows[bass.ts(2 * turn + q, 2 * P), :] if m == P else pair_rows[2 * SEQ:2 * T, :]
                sp.wait_ge(y_stored[q], 16 * turn)
                sp.dma_start(ypair[q][0:m, :], src.rearrange("(t c) d -> t (c d)", c=2)).then_inc(pair_in[q], 16)

            every = sp.to_reg(16 * np2)
            sp.wait_ge(in_filler, 16)
            sp.wait_ge(state_moved, 16)
            sp.wait_ge(rows_out[0], every)
            sp.wait_ge(rows_out[1], every)
            with sp.Fori(0, LAST // 2) as turn:
                for q in range(2):
                    load_pairs(turn, q)
            load_pairs(LAST // 2, 0, NS)

        @block.gpsimd
        def _(pool):
            pool.memset(wst_s[:, :, :], 0.0).then_inc(zeroed, 1)
            pool.memset(xg[0][:, :].bitcast(I32), NOWHERE).then_inc(filled, 1)
            pool.memset(xg[1][:, :], 0.0).then_inc(filled, 1)
            pool.memset(ones[:, :], 1.0).then_inc(filled, 1)
            pool.memset(logits[:, :, :], 0.0).then_inc(filled, 1)
            pool.wait_ge(in_small, 16 * len(small))
            for w, m in ((wst, P), (wst_s, NS)):
                pool.affine_select(out=w[0:m, :, :], in_=w[0:m, :, :], compare_op=ALU.is_ge, fill=0.0,
                                   base=0, pattern=[[0, HEADS], [1, m]], channel_multiplier=-1)\
                    .then_inc(wst_masked, 1)

            pool.wait_ge(in_filler, 16)
            pool.wait_ge(rt, rt_at["table"])
            for j in range(NT):
                m = P if j < LAST else NS
                for c in range(2):
                    pool.indirect_dma_start(
                        slot_table, bass.IndirectOffsetOnAxis(ap=dest[0:m, j, c:c + 1], axis=0),
                        ids[0:m, j, c, :], None, bounds_check=TB * P - 1, oob_is_err=False)\
                        .then_inc(table_stored, 16)
            pool.memset(xg[0][:, :], 0.0).then_inc(filled, 1)
            pool.wait_ge(filled, 5)
            pool.wait_ge(h2_stored, 16 * NT)
            pool.wait_ge(table_stored, 16 * 2 * NT)

            def fetch(b, s, turn):
                pool.dma_start(slot[s][:, :], slot_table[bass.ts(b, P), :]).then_inc(slot_in[s], 16)
                turn = pool.to_reg(turn)
                pool.wait_ge(filled, 5)
                pool.wait_ge(slot_in[s], turn)
                pool.indirect_dma_start(
                    xg[s][:, :], None, h2_rows,
                    bass.IndirectOffsetOnAxis(ap=slot[s][:, 0:1].bitcast(mybir.dt.uint32), axis=0),
                    bounds_check=last_token, oob_is_err=False).then_inc(rows_in[s], 16)

            np2 = pool.value_load(plan[0:1, MAXB:MAXB + 1], min_val=MINB // 2, max_val=MAXB // 2)
            last_token, last_pair = pool.to_reg(T - 1), pool.to_reg(2 * T - 1)
            fetch(0, 0, 16)
            fetch(1, 1, 16)
            with pool.Fori(0, np2) as h:
                for s in range(2):
                    count = pool.to_reg(2 * h + s + 1)
                    pool.wait_ge(table_stored, 16 * 2 * NT)
                    pool.wait_ge(y_ready, count)
                    pool.indirect_dma_start(
                        pair_rows, bass.IndirectOffsetOnAxis(ap=slot[s][:, 1:2].bitcast(mybir.dt.uint32), axis=0),
                        ys[s][:, :], None, bounds_check=last_pair, oob_is_err=False).then_inc(rows_out[s], 16)
                    pool.wait_ge(rows_out[s], 16 * h + 16)
                    fetch(2 * h + s + 2, s, 16 * h + 32)
            for s in range(2):
                pool.wait_ge(rows_in[s], 16 * np2 + 16)

        @block.scalar
        def _(act):
            def square1(i, m, x):
                reached(act, rs1, i)
                act.activation(junk[0:m, :], x, ACT.Square, accum_out=ss1[0:m, 0:1]).then_inc(sq1, 1)

            def step(i, cur, prev, nxt):
                if nxt:
                    m = m_of(nxt)
                    if isinstance(i, int) and i == 0:
                        act.wait_ge(in_x, 32)
                    square1(i + 1, m, xres[0:m, i + 1, :])
                if cur:
                    m = m_of(cur)
                    act.wait_ge(proj_v, i + 1)
                    reached(act, v_ready, i)
                    act.activation(vg[0:m, :], ps[0:m, 2, :], ACT.Gelu).then_inc(v_gelu, 1)
                    act.wait_ge(proj_u, i + 1)
                    reached(act, ya_ready, i)
                    act.activation(u[0:m, :], ps[0:m, 3, :], ACT.Gelu).then_inc(u_gelu, 1)
                    act.wait_ge(proj_p, i + 1)
                    reached(act, ptail_ready, i)
                    if cur == "sample":
                        act.wait_ge(p7_stored, 16)
                    act.activation(p[0:m, :], ps[0:m, 4, :], ACT.Copy).then_inc(p_copied, 1)
                if prev:
                    m = m_of(prev)
                    act.wait_ge(x2_ready, i)
                    reached(act, rs2, i - 1)
                    act.activation(junk[0:m, :], xres[0:m, i - 1, :], ACT.Square,
                                   accum_out=ss2[0:m, 0:1]).then_inc(sq2, 1)
                if cur:
                    m = m_of(cur)
                    act.wait_ge(yaT_done, i + 1)
                    act.activation(yT[:, 0:HEADS, 0:m],
                                   ps[:, 5, :].rearrange("p (k n) -> p k n", n=P)[:, :, 0:m],
                                   ACT.Copy).then_inc(yaT_ready, 1)

            act.wait_ge(in_x0, 16)
            square1(0, P, xres[:, 0, :])
            step(0, "first", None, "mid")
            with act.Fori(1, LAST - 1) as i:
                step(i, "mid", "mid", "mid")
            drain(step)

            act.wait_ge(rt, rt_at["d1"])
            act.activation(rd[:, :, 0:NG], rd[:, :, 0:NG], ACT.Exp).then_inc(rt_exp, 1)
            act.wait_ge(rt, rt_at["d2"])
            act.activation(rv[:, 4, :], rv[:, 3, :], ACT.Exp).then_inc(rt_exp, 1)

            act.wait_ge(rt, rt_at["plan"])
            np2 = act.value_load(plan[0:1, MAXB:MAXB + 1], min_val=MINB // 2, max_val=MAXB // 2)
            with act.Fori(0, np2) as h:
                for s in range(2):
                    b = 2 * h + s
                    act.wait_ge(up1, b + 1)
                    act.wait_ge(hh_ready, b)
                    act.activation(s1[:, :], ps[:, 2, :], ACT.Silu).then_inc(silu_done, 1)
                    act.wait_ge(down, b + 1)
                    act.wait_ge(slot_in[s], 16 * h + 16)
                    act.wait_ge(rows_out[s], 16 * h)
                    act.activation(ys[s][:, :], ps[:, 5:7, :].rearrange("p a n -> p (a n)"), ACT.Copy,
                                   scale=slot[s][:, 2:3].bitcast(F32)).then_inc(y_ready, 1)

            def finish(j, turn, q, m, dst):
                act.wait_ge(x3_ready, j + 1)
                reached(act, rs3, j)
                act.activation(junk[0:m, :], xres[0:m, j, :], ACT.Square,
                               accum_out=ss1[0:m, 0:1]).then_inc(sq3, 1)
                act.wait_ge(y_out, j + 1)
                act.dma_start(dst, ypair[q][0:m, 0:D]).then_inc(y_stored[q], 16)

            with act.Fori(0, LAST // 2) as turn:
                for q in range(2):
                    finish(2 * turn + q, turn, q, P, y_prompt[0, bass.ts(2 * turn + q, P), :])
            finish(LAST, LAST // 2, 0, NS, y_sample.rearrange("b s d -> (b s) d"))
            act.wait_ge(y_stored[0], 16 * (LAST // 2 + 1))
            act.wait_ge(y_stored[1], 16 * (LAST // 2))

        @block.vector
        def _(dve):
            def rstd(w, src, scale, step, turn, done):
                a, y, t = w[:, 2:3], w[:, 1:2], w[:, 3:4]
                chain = [lambda: dve.tensor_scalar(a, src, scale, EPS, ALU.mult, ALU.add),
                         lambda: dve.tensor_scalar(t.bitcast(I32), a.bitcast(I32), 1, None,
                                                   ALU.arith_shift_right),
                         lambda: dve.tensor_scalar(y.bitcast(I32), t.bitcast(I32), -1.0, float(0x5f3759df),
                                                   ALU.mult, ALU.add)]
                for _ in range(3):
                    chain += [lambda: dve.scalar_tensor_tensor(t, y, a, y, ALU.mult, ALU.mult),
                              lambda: dve.tensor_scalar(t, t, -0.5, 1.5, ALU.mult, ALU.add),
                              lambda: dve.tensor_tensor(y, y, t, ALU.mult)]
                assert len(chain) == RSTEPS + 1
                for n, op in enumerate(chain[:-1]):
                    op().then_inc(step, 1)
                    dve.wait_ge(step, RSTEPS * turn + n + 1)
                chain[-1]().then_inc(done, 1)

            def norm1(i, m, x):
                dve.wait_ge(sq1, i + 1)
                rstd(ss1[0:m, :], ss1[0:m, 0:1], 1.0 / D, rs1_step, i, rs1)
                dve.wait_ge(rs1, i + 1)
                reached(dve, xT_done, i)
                dve.tensor_scalar(xn[0:m, :], x, ss1[0:m, 1:2], None, ALU.mult).then_inc(xn_ready, 1)

            def take_hT(i, m):
                dve.wait_ge(xT_done, i + 1)
                reached(dve, proj_p, i)
                dve.tensor_tensor(hT[:, :, 0:m], wide[:, :, 0:m],
                                  g1t[:, :].unsqueeze(2).to_broadcast([P, KD, m]), ALU.mult)\
                    .then_inc(hT_ready, 1)

            def step(i, cur, prev, nxt):
                if nxt:
                    norm1(i + 1, m_of(nxt), xres[0:m_of(nxt), i + 1, :])
                if cur:
                    m = m_of(cur)
                    dve.wait_ge(v_gelu, i + 1)
                    dve.bn_stats(lnst[0:m, 0:6], vg[0:m, :]).then_inc(ln_step, 1)
                    stats = dve.to_reg(4 * i + 1)
                    dve.wait_ge(in_small, 16 * len(small))
                    dve.wait_ge(ln_step, stats)
                    dve.bn_aggr(lnst[0:m, 6:8], lnst[0:m, 0:6]).then_inc(ln_step, 1)
                    dve.wait_ge(ln_step, 4 * i + 2)
                    rstd(lnst[0:m, 8:12], lnst[0:m, 7:8], 1.0, ln_rs_step, i, ln_rs)
                    dve.wait_ge(ln_rs, i + 1)
                    reached(dve, z_done, i)
                    dve.tensor_scalar(v[0:m, :], vg[0:m, :], lnst[0:m, 6:7], lnst[0:m, 9:10],
                                      ALU.subtract, ALU.mult).then_inc(ln_step, 1)
                    dve.wait_ge(ln_step, 4 * i + 3)
                    dve.tensor_tensor(v[0:m, :], v[0:m, :], ag[0:m, :], ALU.mult).then_inc(ln_step, 1)
                    dve.wait_ge(ln_step, 4 * i + 4)
                    dve.tensor_tensor(v[0:m, :], v[0:m, :], ab[0:m, :], ALU.add).then_inc(v_ready, 1)
                if prev:
                    m = m_of(prev)
                    dve.wait_ge(out_a, i)
                    dve.tensor_tensor(xres[0:m, i - 1, 0:512], xres[0:m, i - 1, 0:512], ps[0:m, 6, :],
                                      ALU.add).then_inc(x2a_ready, 1)
                    dve.wait_ge(out_b, i)
                    dve.tensor_tensor(xres[0:m, i - 1, 512:D], xres[0:m, i - 1, 512:D], ps[0:m, 7, :],
                                      ALU.add).then_inc(x2_ready, 1)
                    dve.wait_ge(sq2, i)
                    rstd(ss2[0:m, :], ss2[0:m, 0:1], 1.0 / D, rs2_step, i - 1, rs2)
                    dve.wait_ge(rs2, i)
                    reached(dve, x2T_done, i - 1)
                    reached(dve, h2_stored, 16 * (i - 1))
                    dve.tensor_scalar(xn2[0:m, :], xres[0:m, i - 1, :], ss2[0:m, 1:2], None, ALU.mult)\
                        .then_inc(x2n_ready, 1)
                if nxt:
                    take_hT(i + 1, m_of(nxt))
                if cur:
                    m = m_of(cur)
                    dve.wait_ge(pooled, i + 1)
                    reached(dve, yb_done, i)
                    dve.tensor_copy(poolT[:, :, 0:m],
                                    ps[:, 6, :].rearrange("p (g n) -> p g n", n=P)[:, :, 0:m])\
                        .then_inc(poolT_ready, 1)
                    dve.tensor_copy(ptail[0:m, :], p[0:m, :]).then_inc(ptail_ready, 1)
                    dve.wait_ge(z_done, i + 1)
                    dve.wait_ge(u_gelu, i + 1)
                    reached(dve, yaT_done, i)
                    bias = bst_s if cur == "sample" else bst
                    for h in range(HEADS):
                        c = slice(h * P, (h + 1) * P)
                        last = dve.scalar_tensor_tensor(ya[0:m, c], ps[0:m, 5, c], bias[0:m, h:h + 1],
                                                        u[0:m, c], ALU.add, ALU.mult)
                    last.then_inc(ya_ready, 1)
                if prev:
                    m = m_of(prev)
                    dve.wait_ge(x2T_done, i)
                    reached(dve, logit_done, i - 1)
                    dve.tensor_tensor(h2T[:, :, 0:m], wide[:, :, 0:m],
                                      g2t[:, :].unsqueeze(2).to_broadcast([P, KD, m]), ALU.mult)\
                        .then_inc(h2T_ready, 1)
                if cur:
                    m = m_of(cur)
                    dve.wait_ge(yb_done, i + 1)
                    reached(dve, out_b, i)
                    dve.tensor_tensor(yT[:, HEADS:KD, 0:m],
                                      ps[:, 6, :].rearrange("p (g n) -> p g n", n=P)[:, :, 0:m],
                                      bsc[:, :].unsqueeze(2).to_broadcast([P, GROUPS, m]), ALU.mult)\
                        .then_inc(ybT_ready, 1)
                if prev:
                    m = m_of(prev)
                    dve.wait_ge(logit_done, i)
                    if isinstance(i, int) and i == 1:
                        dve.wait_ge(filled, 4)
                    dve.tensor_tensor(logits[0:m, i - 1, :], ps[0:m, 7, 0:NR], rb[0:m, :], ALU.add)\
                        .then_inc(logits_ready, 1)

            dve.wait_ge(in_x0, 16)
            norm1(0, P, xres[:, 0, :])
            dve.wait_ge(in_first, 32)
            take_hT(0, P)
            step(0, "first", None, "mid")
            dve.wait_ge(filled, 4)
            with dve.Fori(1, LAST - 1) as i:
                step(i, "mid", "mid", "mid")
            drain(step)

            def link(ins, name=None):
                rt_steps.append(1)
                ins.then_inc(rt, 1)
                dve.wait_ge(rt, len(rt_steps))
                if name:
                    assert rt_at[name] == len(rt_steps), (name, len(rt_steps))

            rt_steps = []
            l1, l2 = logits[:, :, 0:NG], logits[:, :, NG:NR]
            rev4 = crow[:, 0:NG].unsqueeze(1).to_broadcast([P, NT, NG])
            rev32 = crow[:, NG:NR].unsqueeze(1).to_broadcast([P, NT, NE])

            def over(x, n):
                return x.unsqueeze(2).to_broadcast([P, NT, n])

            dve.wait_ge(logits_ready, NT)
            link(dve.tensor_reduce(rv[:, 0, :], l1, AX, ALU.max))
            link(dve.tensor_tensor(rd[:, :, 0:NG], l1, over(rv[:, 0, :], NG), ALU.subtract), "d1")
            link(dve.tensor_tensor(ra[:, :, 0:NG], l1, over(rv[:, 0, :], NG), ALU.is_equal))
            link(dve.tensor_tensor(ra[:, :, 0:NG], ra[:, :, 0:NG], rev4, ALU.mult))
            link(dve.tensor_reduce(rv[:, 1, :], ra[:, :, 0:NG], AX, ALU.max))
            link(dve.tensor_tensor(ra[:, :, 0:NG], over(rv[:, 1, :], NG), rev4, ALU.is_equal))
            link(dve.tensor_scalar(ra[:, :, NG:2 * NG], ra[:, :, 0:NG], 1.0, BIG, ALU.subtract, ALU.mult))

            for j in range(NT):
                link(dve.tensor_tensor(rm[:, j, :].rearrange("p (g e) -> p g e", e=EPG),
                                       l2[:, j, :].rearrange("p (g e) -> p g e", e=EPG),
                                       ra[:, j, 0:NG].unsqueeze(2).to_broadcast([P, NG, EPG]), ALU.mult))
                link(dve.tensor_tensor(rm[:, j, :].rearrange("p (g e) -> p g e", e=EPG),
                                       rm[:, j, :].rearrange("p (g e) -> p g e", e=EPG),
                                       ra[:, j, NG:2 * NG].unsqueeze(2).to_broadcast([P, NG, EPG]), ALU.add))
            for c, oh in enumerate((oh1, oh2)):
                link(dve.tensor_reduce(rv[:, 1 + c, :], rm[:, :, :], AX, ALU.max))
                link(dve.tensor_tensor(oh[:, :, :], rm[:, :, :], over(rv[:, 1 + c, :], NE), ALU.is_equal))
                link(dve.tensor_tensor(oh[:, :, :], oh[:, :, :], rev32, ALU.mult))
                link(dve.tensor_reduce(rv[:, 5, :], oh[:, :, :], AX, ALU.max))
                link(dve.tensor_tensor(oh[:, :, :], over(rv[:, 5, :], NE), rev32, ALU.is_equal))
                if c == 0:
                    link(dve.scalar_tensor_tensor(rm[:, :, :], oh[:, :, :], -2.0 * BIG, rm[:, :, :],
                                                  ALU.mult, ALU.add))
            link(dve.tensor_tensor(rv[:, 3, :], rv[:, 2, :], rv[:, 1, :], ALU.subtract), "d2")
            link(dve.tensor_tensor(mk[:, :, :], oh1[:, :, :], oh2[:, :, :], ALU.add))
            link(dve.memset(mk[NS:P, LAST, :], 0.0), "mask")
            dve.wait_ge(rt_exp, 2)
            link(dve.tensor_reduce(rv[:, 5, :], rd[:, :, 0:NG], AX, ALU.add))
            link(dve.tensor_scalar(rv[:, 6, :], rv[:, 4, :], 1.0, None, ALU.add))
            link(dve.tensor_tensor(rv[:, 5, :], rv[:, 5, :], rv[:, 6, :], ALU.mult))
            link(dve.reciprocal(rv[:, 6, :], rv[:, 5, :]))
            link(dve.tensor_copy(ids[:, :, 0, 2].bitcast(F32), rv[:, 6, :]))
            link(dve.tensor_tensor(ids[:, :, 1, 2].bitcast(F32), rv[:, 6, :], rv[:, 4, :], ALU.mult))
            dve.wait_ge(rt_rank, 2)
            tot = ps[:, 6, 0:NT * NE].rearrange("p (j e) -> p j e", e=NE)
            link(dve.memset(base[:, 0, :], 0.0))
            for j in range(NT):
                link(dve.tensor_tensor(base[:, j + 1, :], base[:, j, :], tot[:, j, :], ALU.add))
            link(dve.tensor_tensor(cmp[:, 0:NE * THRESH].rearrange("p (e k) -> p e k", k=THRESH),
                                   base[:, NT, :].unsqueeze(2).to_broadcast([P, NE, THRESH]),
                                   crow[:, NR + MAXB:].unsqueeze(1).to_broadcast([P, NE, THRESH]),
                                   ALU.is_gt))
            link(dve.tensor_reduce(blk[:, 0, :], cmp[:, 0:NE * THRESH].rearrange("p (e k) -> p e k", k=THRESH),
                                   AX, ALU.add))
            link(dve.memset(blk[:, 2, :], 1.0))
            link(dve.tensor_tensor_scan(blk[:, 1, :], blk[:, 2, :], blk[:, 0, :], 0.0, ALU.mult, ALU.add))
            link(dve.tensor_tensor(blk[:, 2, :], blk[:, 1, :], blk[:, 0, :], ALU.subtract))
            link(dve.tensor_scalar(blk[:, 2, :], blk[:, 2, :], float(P), None, ALU.mult))
            link(dve.tensor_tensor(cmp[0:1, :].rearrange("p (b e) -> p b e", e=NE),
                                   blk[0:1, 1, :].unsqueeze(1).to_broadcast([1, MAXB, NE]),
                                   crow[0:1, NR:NR + MAXB].unsqueeze(2).to_broadcast([1, MAXB, NE]),
                                   ALU.is_le))
            link(dve.tensor_reduce(planf[0:1, 0:MAXB], cmp[0:1, :].rearrange("p (b e) -> p b e", e=NE),
                                   AX, ALU.add))
            link(dve.tensor_scalar(planf[0:1, 0:MAXB], planf[0:1, 0:MAXB], float(NE - 1), None, ALU.min))
            link(dve.tensor_scalar(cmp[0:1, 0:MAXB // 2], crow[0:1, NR:NR + MAXB:2], blk[0:1, 1, NE - 1:NE], None,
                                   ALU.is_lt))
            link(dve.tensor_reduce(planf[0:1, MAXB:MAXB + 1], cmp[0:1, 0:MAXB // 2], AX, ALU.add))
            link(dve.tensor_copy(plan[0:1, :], planf[0:1, :]), "plan")
            link(dve.tensor_tensor(mk[:, :, :], ps[:, 5, 0:NT * NE].rearrange("p (j e) -> p j e", e=NE),
                                   base[:, 0:NT, :], ALU.add))
            link(dve.tensor_tensor(mk[:, :, :], mk[:, :, :],
                                   blk[:, 2, :].unsqueeze(1).to_broadcast([P, NT, NE]), ALU.add))
            for c, oh in enumerate((oh1, oh2)):
                link(dve.tensor_tensor(oh[:, :, :], oh[:, :, :], mk[:, :, :], ALU.mult))
                link(dve.tensor_reduce(rv[:, c, :], oh[:, :, :], AX, ALU.add))
                link(dve.tensor_copy(dest[:, :, c].bitcast(I32), rv[:, c, :]), "table" if c else None)

            def take_xgT(b):
                dve.wait_ge(xgT_done, b + 1)
                dve.tensor_tensor(xT[:, :, :], wide, g2t[:, :].unsqueeze(2).to_broadcast([P, KD, P]),
                                  ALU.mult).then_inc(xgT_ready, 1)

            np2 = dve.value_load(plan[0:1, MAXB:MAXB + 1], min_val=MINB // 2, max_val=MAXB // 2)
            take_xgT(0)
            with dve.Fori(0, np2) as h:
                for s in range(2):
                    b = 2 * h + s
                    dve.wait_ge(silu_done, b + 1)
                    dve.wait_ge(up3, b + 1)
                    dve.wait_ge(hhT_done, b)
                    dve.tensor_tensor(hh[:, :], s1[:, :], ps[:, 3, :], ALU.mult).then_inc(hh_ready, 1)
                    take_xgT(b + 1)
                    dve.wait_ge(hhT_done, b + 1)
                    dve.wait_ge(down, b)
                    dve.tensor_copy(hhT[:, :, :], ps[:, 4, :].rearrange("p (k n) -> p k n", n=P))\
                        .then_inc(hhT_ready, 1)

            def finish(j, turn, q, m):
                yp = ypair[q]
                dve.wait_ge(pair_in[q], 16 * turn + 16)
                dve.tensor_tensor(yp[0:m, 0:D], yp[0:m, 0:D], yp[0:m, D:2 * D], ALU.add).then_inc(pair_sum, 1)
                dve.wait_ge(pair_sum, j + 1)
                dve.tensor_tensor(xres[0:m, j, :], xres[0:m, j, :], yp[0:m, 0:D], ALU.add).then_inc(x3_ready, 1)
                dve.wait_ge(sq3, j + 1)
                rstd(ss1[0:m, :], ss1[0:m, 0:1], 1.0 / D, rs3_step, j, rs3)
                dve.wait_ge(rs3, j + 1)
                dve.scalar_tensor_tensor(yp[0:m, 0:D], xres[0:m, j, :], ss1[0:m, 1:2], gf[0:m, :],
                                         ALU.mult, ALU.mult).then_inc(y_out, 1)

            with dve.Fori(0, LAST // 2) as turn:
                for q in range(2):
                    finish(2 * turn + q, turn, q, P)
            finish(LAST, LAST // 2, 0, NS)

        @block.tensor
        def _(pe):
            def turn(x, m, done, k=KD, bank=0):
                xs = x[0:m, :].rearrange("t (p k) -> t k p", k=k)
                for c in range(k):
                    last = pe.transpose(ps[:, bank + c // 4, (c % 4) * P:(c % 4) * P + m], xs[:, c, :],
                                        ident[0:m, 0:m])
                last.then_inc(done, 1)

            def step(i, cur, prev, nxt):
                if cur:
                    m = m_of(cur)
                    pe.wait_ge(hT_ready, i + 1)
                    for bank, part, free, done in ((2, 1, v_gelu, proj_v), (3, 0, u_gelu, proj_u),
                                                   (4, 2, p_copied, proj_p)):
                        reached(pe, free, i)
                        for k in range(KD):
                            if isinstance(i, int) and i == 0 and bank == 2 and k % 2 == 0:
                                pe.wait_ge(in_win[k // 2], 16)
                            last = pe.matmul(ps[0:m, bank, :], hT[:, k, 0:m], win[:, k, part * AW:(part + 1) * AW],
                                             start=(k == 0), stop=(k == KD - 1))
                        last.then_inc(done, 1)
                if prev:
                    m = m_of(prev)
                    if isinstance(i, int) and i == 1:
                        pe.wait_ge(in_wout, 32)
                    pe.wait_ge(yaT_ready, i)
                    pe.wait_ge(ybT_ready, i)
                    reached(pe, logits_ready, i - 1)
                    for half, done in ((0, out_a), (1, out_b)):
                        for k in range(KD):
                            last = pe.matmul(ps[0:m, 6 + half, :], yT[:, k, 0:m],
                                             wout[:, k, half * 512:(half + 1) * 512],
                                             start=(k == 0), stop=(k == KD - 1))
                        last.then_inc(done, 1)
                if nxt:
                    pe.wait_ge(xn_ready, i + 2)
                    reached(pe, h2T_ready, i - 1)
                    turn(xn, m_of(nxt), xT_done)
                if cur:
                    m = m_of(cur)
                    w = wst_s if cur == "sample" else wst
                    pe.wait_ge(v_ready, i + 1)
                    if isinstance(i, int) and i == 0:
                        pe.wait_ge(wst_masked, 2)
                    for h in range(HEADS):
                        last = pe.matmul(ps[0:m, 5, h * P:(h + 1) * P], w[0:m, h, 0:m],
                                         v[0:m, h * P:(h + 1) * P], start=True, stop=True)
                    last.then_inc(z_done, 1)
                    pe.wait_ge(p_copied, i + 1)
                    reached(pe, ptail_ready, i)
                    reached(pe, x2a_ready, i)
                    parts = {"first": [(p, band_first, P)], "mid": [(p, band, P), (ptail, band_prev, P)],
                             "sample": [(p, band_s, NS), (state, band_state, DEC * STATE)]}[cur]
                    for g in range(GROUPS):
                        for n, (src, bnd, kk) in enumerate(parts):
                            last = pe.matmul(ps[:, 6, g * P:g * P + m], src[0:kk, g * P:(g + 1) * P],
                                             bnd[0:kk, g, 0:m], start=(n == 0), stop=(n == len(parts) - 1))
                    last.then_inc(pooled, 1)
                if prev:
                    pe.wait_ge(x2n_ready, i)
                    if nxt:
                        pe.wait_ge(hT_ready, i + 2)
                    turn(xn2, m_of(prev), x2T_done)
                if cur:
                    m = m_of(cur)
                    pe.wait_ge(poolT_ready, i + 1)
                    for g in range(GROUPS):
                        last = pe.matmul(ps[:, 6, g * P:g * P + m], bw[:, g, :], poolT[:, g, 0:m],
                                         start=True, stop=True)
                    last.then_inc(yb_done, 1)
                    pe.wait_ge(ya_ready, i + 1)
                    turn(ya, m, yaT_done, HEADS, 5)
                if prev:
                    m = m_of(prev)
                    pe.wait_ge(h2T_ready, i)
                    for k in range(KD):
                        last = pe.matmul(ps[0:m, 7, 0:NR], h2T[:, k, 0:m], rw[:, k, :],
                                         start=(k == 0), stop=(k == KD - 1))
                    last.then_inc(logit_done, 1)

            pe.wait_ge(in_first, 32)
            pe.wait_ge(xn_ready, 1)
            turn(xn, P, xT_done)
            step(0, "first", None, "mid")
            pe.wait_ge(in_wout, 32)
            with pe.Fori(1, LAST - 1) as i:
                step(i, "mid", "mid", "mid")
            drain(step)

            pe.wait_ge(rt, rt_at["mask"])
            mkf = mk[:, :, :].rearrange("p j e -> p (j e)")
            pe.matmul(ps[:, 5, 0:NT * NE], tri[:, :], mkf, start=True, stop=True).then_inc(rt_rank, 1)
            pe.matmul(ps[:, 6, 0:NT * NE], ones[:, :], mkf, start=True, stop=True).then_inc(rt_rank, 1)

            pe.wait_ge(rt, rt_at["table"])
            np2 = pe.value_load(plan[0:1, MAXB:MAXB + 1], min_val=MINB // 2, max_val=MAXB // 2)
            pe.wait_ge(rows_in[0], 16)
            turn(xg[0], P, xgT_done)
            with pe.Fori(0, np2) as h:
                for s in range(2):
                    b = 2 * h + s
                    pe.wait_ge(xgT_ready, b + 1)
                    for bank, w, w_in_sem, done in ((2, ew1[s], w1_in[s], up1), (3, ew3[s], w3_in[s], up3)):
                        pe.wait_ge(w_in_sem, 16 * h + 16)
                        for k in range(KD):
                            last = pe.matmul(ps[:, bank, :], xT[:, k, :], w[:, k, :],
                                             start=(k == 0), stop=(k == KD - 1))
                        last.then_inc(done, 1)
                    pe.wait_ge(rows_in[1 - s], 16 * h + (32 if s else 16))
                    turn(xg[1 - s], P, xgT_done)
                    pe.wait_ge(hh_ready, b + 1)
                    turn(hh, P, hhT_done, KF, 4)
                    pe.wait_ge(hhT_ready, b + 1)
                    pe.wait_ge(w2_in[s], 16 * h + 16)
                    pe.wait_ge(y_ready, b)
                    for half in range(2):
                        for k in range(KF):
                            last = pe.matmul(ps[:, 5 + half, :], hhT[:, k, :],
                                             ew2[s][:, k, half * 512:(half + 1) * 512],
                                             start=(k == 0), stop=(k == KF - 1))
                    last.then_inc(down, 1)


def constants():
    import numpy as np
    f = np.float32
    s, t = np.arange(P)[:, None], np.arange(P)[None, :]
    w = np.array(WINDOWS)[None, :, None]
    d = (t - s)[:, None, :]
    own = -(d == 0).astype(f)
    c = {"ident": np.eye(P, dtype=f), "tri": (s < t).astype(f)}
    inside = ((d >= 0) & (d < w)).astype(f)
    c["band"] = inside / w.astype(f) + own
    c["band_first"] = inside / np.minimum(t[:, None, :] + 1, w).astype(f) + own
    c["band_prev"] = ((d + P < w).astype(f) / w.astype(f))
    q, r = np.arange(NS) // DSEQ, np.arange(NS) % DSEQ
    same = (q[:, None] == q[None, :])[:, None, :]
    c["band_s"] = (same * c["band"][:NS, :, :NS]).astype(f)
    sq, sr = np.arange(DEC * STATE) // STATE, np.arange(DEC * STATE) % STATE
    ds = (STATE + r[None, :] - sr[:, None])[:, None, :]
    c["band_state"] = ((sq[:, None] == q[None, :])[:, None, :] * (ds < w) / w).astype(f)
    c["row"] = np.concatenate([NG - np.arange(NG), NE - np.arange(NE), np.arange(MAXB),
                               P * np.arange(THRESH)]).astype(f)
    ids = np.zeros((P, NT, 2, 4), np.int32)
    tok = np.arange(P)[:, None] + P * np.arange(NT)[None, :]
    for k in range(2):
        ids[:, :, k, 0] = tok
        ids[:, :, k, 1] = 2 * tok + k
    c["ids"] = ids
    return {k: np.ascontiguousarray(v) for k, v in c.items()}


def kernel(**inputs):
    import numpy as np
    import concourse.bacc as bacc
    from concourse.bass_utils import run_bass_kernel_spmd

    a = {k: np.ascontiguousarray(v) for k, v in inputs.items()}
    host = {k: a[k] for k in ("x_prompt", "x_sample", "state_pool", "norm1_g", "w_in", "a_norm_g", "a_norm_b")}
    host["ws_sht"] = np.ascontiguousarray(a["a_ws"][0].transpose(2, 0, 1))
    host["bs_th"] = np.ascontiguousarray(a["a_bs"][0].transpose(1, 0))
    host["bsc_dg"] = np.ascontiguousarray(a["b_scale"][0].reshape(GROUPS, P).T)
    host.update({k: a[k] for k in ("b_w", "w_out", "norm2_g")})
    host["r_w"] = np.concatenate([a["r1_w"][0], a["r2_w"][0].transpose(1, 0, 2).reshape(D, NE)], axis=1)
    host["r_b"] = np.concatenate([a["r1_b"][0], a["r2_b"][0].reshape(NE)])
    host.update({k: a[k] for k in ("exp_w1", "exp_w3", "exp_w2", "normf_g")})
    host.update({f"c_{k}": v for k, v in constants().items()})
    order = ["x_prompt", "x_sample", "state_pool", "norm1_g", "w_in", "a_norm_g", "a_norm_b", "ws_sht", "bs_th",
             "b_w", "bsc_dg", "w_out", "norm2_g", "r_w", "r_b", "exp_w1", "exp_w3", "exp_w2", "normf_g",
             "c_ident", "c_band", "c_band_first", "c_band_prev", "c_band_s", "c_band_state", "c_tri", "c_row", "c_ids"]

    nc = bacc.Bacc("TRN2", target_bir_lowering=False, num_devices=1)
    arrays, args = {}, []
    for name in order:
        x = np.ascontiguousarray(host[name])
        arrays[f"in_{name}"] = x
        args.append(nc.dram_tensor(f"in_{name}", x.shape, mybir.dt.from_np(x.dtype), kind="ExternalInput").ap())
    outs = [("y_prompt", (1, SEQ, D)), ("y_sample", (DEC, DSEQ, D)), ("pool_p", (1, 1, STATE, AW)),
            ("pool_s", (1, DEC, STATE, AW)), ("v_s", (1, DEC, DSEQ, AW))]
    for name, shape in outs:
        args.append(nc.dram_tensor(f"out_{name}", shape, F32, kind="ExternalOutput").ap())
    build(nc, *args)
    r = run_bass_kernel_spmd(nc, [arrays], core_ids=[0])
    return tuple(r.results[0][f"out_{name}"] for name, _ in outs)
```

```python
from contextlib import ExitStack

import concourse.bass as bass
from concourse import mybir

P = 128
D = 1024
SEQ = 1024
NS = 64
DEC, DSEQ = 8, 8
T = SEQ + NS
NT = SEQ // P + 1
KD = D // P
AW = 512
HEADS = GROUPS = 4
STATE = 15
WINDOWS = (2, 4, 8, 16)
TAIL = 32
NG, NE, EPG = 4, 32, 8
NR = NG + NE
FE = 512
KF = FE // P
REG = -(-T // P) * P
OVER = 8
MAXO = 16
CH = 6
CHW = 2048
EPS = 1e-6
BIG = 1.0e30
NOWHERE = 1 << 14

F32 = mybir.dt.float32
I32 = mybir.dt.int32
U32 = mybir.dt.uint32
ALU = mybir.AluOpType
ACT = mybir.ActivationFunctionType
AX = mybir.AxisListType.X


def reached(eng, sem, n):
    if not isinstance(n, int) or n > 0:
        eng.wait_ge(sem, n)


def not_first(h, s=0):
    return not (isinstance(h, int) and h == 0) or s > 0


def build(nc, x_prompt, x_sample, state_pool, norm1_g, w_in, a_norm_g, a_norm_b, ws_sht, bs_th,
          b_w, bsc_dg, w_out, norm2_g, r_w, r_b, exp_w1, exp_w3, exp_w2, normf_g,
          c_ident, c_band, c_band_first, c_band_prev, c_band_s, c_band_state, c_tri, c_row, c_base, c_ids,
          y_prompt, y_sample, pool_p, pool_s, v_s):
    ctx = ExitStack()
    with ctx:
        def sb(name, shape, dt=F32):
            return ctx.enter_context(nc.sbuf_tensor(name, shape, dt))

        def sem(name):
            return ctx.enter_context(nc.semaphore(name))

        h2_rows = nc.dram_tensor("h2_rows", [T, D], F32, kind="Internal").ap()
        pair_rows = nc.dram_tensor("pair_rows", [2 * T, D], F32, kind="Internal").ap()
        slot_table = nc.dram_tensor("slot_table", [NE * REG, 2], I32, kind="Internal").ap()

        xres = sb("xres", [P, NT, D])
        big = sb("big", [P, 2 * CH * CHW])
        win = big[:, 0:KD * 3 * AW].rearrange("p (k n) -> p k n", k=KD)
        wout = big[:, KD * 3 * AW:KD * (3 * AW + D)].rearrange("p (k n) -> p k n", k=KD)
        chunk = [big[:, c * CHW:(c + 1) * CHW] for c in range(2 * CH)]

        ident = sb("ident", [P, P])
        band = sb("band", [P, GROUPS, P])
        band_first = sb("band_first", [P, GROUPS, P])
        band_prev = sb("band_prev", [P, GROUPS, P])
        band_s = sb("band_s", [P, GROUPS, NS])
        band_state = sb("band_state", [P, GROUPS, NS])
        state = sb("state", [P, AW])
        tri = sb("tri", [P, P])
        ones = sb("ones", [P, P])
        wst = sb("wst", [P, HEADS, P])
        wst_s = sb("wst_s", [P, HEADS, NS])
        bst = sb("bst", [P, HEADS])
        bst_s = sb("bst_s", [P, HEADS])
        g1t = sb("g1t", [P, KD])
        g2t = sb("g2t", [P, KD])
        ag = sb("ag", [P, AW])
        ab = sb("ab", [P, AW])
        gf = sb("gf", [P, D])
        bw = sb("bw", [P, GROUPS, P])
        bsc = sb("bsc", [P, GROUPS])
        rw = sb("rw", [P, KD, NR])
        rb = sb("rb", [P, NR])
        crow = sb("crow", [P, NG + NE + MAXO + OVER])
        ids = sb("ids", [P, NT, 2, 2], I32)
        base = sb("base", [P, NE])
        base0 = sb("base0", [P, NE])

        xn = sb("xn", [P, D])
        hT = sb("hT", [P, KD, P])
        u = sb("u", [P, AW])
        vg = sb("vg", [P, AW])
        v = sb("v", [P, AW])
        p = sb("p", [P, AW])
        ptail = sb("ptail", [P, AW])
        poolT = sb("poolT", [P, GROUPS, P])
        ya = sb("ya", [P, AW])
        yT = sb("yT", [P, KD, P])
        xn2 = sb("xn2", [P, D])
        h2T = sb("h2T", [P, KD, P])
        junk = sb("junk", [P, D])
        ss1 = sb("ss1", [P, 4])
        ss2 = sb("ss2", [P, 4])
        ssf = sb("ssf", [P, 4, NT])
        lnst = sb("lnst", [P, 16])
        logits = sb("logits", [P, NR])

        ra = sb("ra", [P, 3 * NG])
        rv = sb("rv", [P, 8])
        rm = sb("rm", [P, NE])
        oh = [sb(f"oh{c}", [P, NE]) for c in range(2)]
        mk = sb("mk", [P, NE])
        rs = sb("rs", [P, NE])
        rd = sb("rd", [P, NT, NG])
        vd = sb("vd", [P, NT])
        gate = [sb(f"gate{c}", [P, NT]) for c in range(2)]
        destf = sb("destf", [P, 2])
        dest = sb("dest", [P, NT, 2], U32)
        cmp = junk[0:1, 0:MAXO * NE].rearrange("p (n e) -> p n e", e=NE)
        blk = sb("blk", [1, 4, NE])
        planf = sb("planf", [1, 2 * MAXO + 1])
        plan = sb("plan", [1, 2 * MAXO + 1], I32)

        tabs = sb("tabs", [P, NE, 2], I32)
        gidx = [sb(f"gidx{s}", [P, 1], I32) for s in range(2)]
        sidx = [sb(f"sidx{s}", [P, 1], I32) for s in range(2)]
        xg = [sb(f"xg{s}", [P, D]) for s in range(2)]
        oidx = sb("oidx", [P, 2], I32)
        xT = hT
        s1 = u
        hh = v
        hhT = poolT
        ys = [xn, xn2]
        ypair = [big[:, j * 2 * D:(j + 1) * 2 * D] for j in range(NT)]

        ps = ctx.enter_context(nc.psum_tensor("ps", [P, 8, 512], F32))
        wide = ps[:, 0:2, :].rearrange("p a (k n) -> p (a k) n", n=P)

        in_first = sem("in_first")
        in_small = sem("in_small")
        in_late = sem("in_late")
        in_x0 = sem("in_x0")
        in_x1 = sem("in_x1")
        in_x = sem("in_x")
        in_win = [sem(f"in_win{q}") for q in range(4)]
        in_wout = sem("in_wout")
        in_filler = sem("in_filler")
        state_moved = sem("state_moved")
        sq1 = sem("sq1")
        rs1 = sem("rs1")
        rs1_step = sem("rs1_step")
        xn_ready = sem("xn_ready")
        xT_done = sem("xT_done")
        hT_ready = sem("hT_ready")
        proj_v = sem("proj_v")
        proj_u = sem("proj_u")
        proj_p = sem("proj_p")
        v_gelu = sem("v_gelu")
        u_gelu = sem("u_gelu")
        p_copied = sem("p_copied")
        ln_step = sem("ln_step")
        ln_rs_step = sem("ln_rs_step")
        ln_rs = sem("ln_rs")
        v_ready = sem("v_ready")
        z_done = sem("z_done")
        pooled = sem("pooled")
        ya_ready = sem("ya_ready")
        poolT_ready = sem("poolT_ready")
        ptail_ready = sem("ptail_ready")
        yb_done = sem("yb_done")
        yaT_done = sem("yaT_done")
        yaT_ready = sem("yaT_ready")
        ybT_ready = sem("ybT_ready")
        out_a = sem("out_a")
        out_b = sem("out_b")
        x2a_ready = sem("x2a_ready")
        x2_ready = sem("x2_ready")
        sq2 = sem("sq2")
        rs2 = sem("rs2")
        rs2_step = sem("rs2_step")
        x2n_ready = sem("x2n_ready")
        h2_stored = sem("h2_stored")
        x2T_done = sem("x2T_done")
        h2T_ready = sem("h2T_ready")
        logit_done = sem("logit_done")
        logits_ready = sem("logits_ready")
        zeroed = sem("zeroed")
        filled = sem("filled")
        wst_masked = sem("wst_masked")
        p7_stored = sem("p7_stored")
        outs = sem("outs")
        r1_step = sem("r1_step")
        mk_ready = sem("mk_ready")
        rank_done = sem("rank_done")
        r2_step = sem("r2_step")
        rank_taken = sem("rank_taken")
        dest_ready = sem("dest_ready")
        table_stored = sem("table_stored")
        gate_exp = sem("gate_exp")
        gate_step = sem("gate_step")
        plan_step = sem("plan_step")
        plan_ready = sem("plan_ready")
        tabs_in = [sem(f"tabs_in{n}") for n in range(2)]
        chunk_in = [sem(f"chunk_in{c}") for c in range(2 * CH)]
        used = sem("used")
        gidx_ready = sem("gidx_ready")
        sidx_ready = sem("sidx_ready")
        rows_in = [sem(f"rows_in{s}") for s in range(2)]
        rows_out = [sem(f"rows_out{s}") for s in range(2)]
        xgT_done = sem("xgT_done")
        xgT_ready = sem("xgT_ready")
        up3a = sem("up3a")
        silu_done = sem("silu_done")
        hha_ready = sem("hha_ready")
        hhb_ready = sem("hhb_ready")
        hhaT_done = sem("hhaT_done")
        hhbT_done = sem("hhbT_done")
        hhaT_ready = sem("hhaT_ready")
        hhbT_ready = sem("hhbT_ready")
        y_ready = sem("y_ready")
        ov_free = sem("ov_free")
        ov_w = sem("ov_w")
        ov_idx = sem("ov_idx")
        ov_rows = sem("ov_rows")
        ov_xT = sem("ov_xT")
        ov_x = sem("ov_x")
        ov_up = sem("ov_up")
        ov_silu = sem("ov_silu")
        ov_hh = sem("ov_hh")
        ov_hT = sem("ov_hT")
        ov_h = sem("ov_h")
        ov_down = sem("ov_down")
        ov_y = sem("ov_y")
        ov_out = sem("ov_out")
        pair_in = [sem(f"pair_in{j}") for j in range(NT)]
        y_stored = sem("y_stored")
        ssf_set = sem("ssf_set")
        pair_sum = sem("pair_sum")
        x3_ready = sem("x3_ready")
        sq3 = sem("sq3")
        rs3 = sem("rs3")
        rs3_step = sem("rs3_step")
        y_out = sem("y_out")

        LAST = NT - 1
        small, late = [], []

        def m_of(kind):
            return NS if kind == "sample" else P

        def pipeline(eng, step):
            step(0, "first", None, None, "mid")
            step(1, "mid", "mid", None, "mid")
            with eng.Fori(2, LAST - 1) as i:
                step(i, "mid", "mid", "mid", "mid")
            step(LAST - 1, "mid", "mid", "mid", "sample")
            step(LAST, "sample", "mid", "mid", None)
            step(LAST + 1, None, "sample", "mid", None)
            step(LAST + 2, None, None, "sample", None)

        block = ctx.enter_context(nc.Block())

        @block.sync
        def _(sp):
            xp = x_prompt[0]

            def load(dst, src):
                small.append(1)
                sp.dma_start(dst, src).then_inc(in_small, 16)

            def load_late(dst, src):
                late.append(1)
                sp.dma_start(dst, src).then_inc(in_late, 16)

            sp.dma_start(xres[:, 0, :], xp[0:P, :]).then_inc(in_x0, 16)
            sp.dma_start(ident[:, :], c_ident).then_inc(in_first, 16)
            sp.dma_start(g1t[:, :], norm1_g[0].rearrange("(p k) -> p k", k=KD)).then_inc(in_first, 16)
            wv = w_in[0].rearrange("(p k) n -> p k n", k=KD)
            for q in range(4):
                sp.dma_start(win[:, 2 * q:2 * q + 2, :], wv[:, 2 * q:2 * q + 2, :]).then_inc(in_win[q], 16)
            load(ag[:, :], a_norm_g[0].partition_broadcast(P))
            load(ab[:, :], a_norm_b[0].partition_broadcast(P))
            load(wst[:, :, :], ws_sht)
            load(bst[:, :], bs_th)
            load(band_first[:, :, :], c_band_first)
            load(bw[:, :, :], b_w[0].rearrange("g c d -> c g d"))
            load(bsc[:, :], bsc_dg)
            sp.dma_start(xres[:, 1, :], xp[P:2 * P, :]).then_inc(in_x1, 16)
            sp.dma_start(wout[:, 0:HEADS, :],
                         w_out[0, 0:AW, :].rearrange("(p k) n -> p k n", k=HEADS)).then_inc(in_wout, 16)
            sp.dma_start(wout[:, HEADS:KD, :],
                         w_out[0, AW:D, :].rearrange("(g d) n -> d g n", g=GROUPS)).then_inc(in_wout, 16)
            load_late(band[:, :, :], c_band)
            load_late(band_prev[:, :, :], c_band_prev)
            load_late(g2t[:, :], norm2_g[0].rearrange("(p k) -> p k", k=KD))
            load_late(rw[:, :, :], r_w.rearrange("(p k) n -> p k n", k=KD))
            load_late(rb[:, :], r_b.partition_broadcast(P))
            load_late(tri[:, :], c_tri)
            load_late(crow[:, :], c_row.partition_broadcast(P))
            load_late(ids[:, :, :, :], c_ids)
            load_late(base[:, :], c_base.partition_broadcast(P))
            load_late(base0[:, :], c_base.partition_broadcast(P))
            load_late(band_s[0:NS, :, :], c_band_s)
            load_late(band_state[0:DEC * STATE, :, :], c_band_state)
            load_late(state[0:DEC * STATE, :], state_pool[0].rearrange("b s c -> (b s) c"))
            load_late(gf[:, :], normf_g.partition_broadcast(P))
            sp.wait_ge(zeroed, 1)
            for b in range(DEC):
                r = slice(b * DSEQ, (b + 1) * DSEQ)
                load_late(wst_s[r, :, r], ws_sht[0:DSEQ, :, 0:DSEQ])
                load_late(bst_s[r, :], bs_th[0:DSEQ, :])
            sp.dma_start(xres[:, 2:NT - 1, :],
                         xp[2 * P:SEQ, :].rearrange("(j p) d -> p j d", p=P)).then_inc(in_x, 16)
            sp.dma_start(xres[0:NS, NT - 1, :], x_sample.rearrange("b s d -> (b s) d")).then_inc(in_x, 16)
            sp.dma_start(pool_s[0, :, 0:STATE - DSEQ, :],
                         state_pool[0, :, DSEQ:STATE, :]).then_inc(state_moved, 16)
            sp.wait_ge(filled, 1)
            sp.dma_start(slot_table.rearrange("(p q) c -> p (q c)", p=P),
                         xg[0][:, 0:NE * REG * 2 // P].bitcast(I32)).then_inc(in_filler, 16)

            def store_h2(i, m=P):
                reached(sp, x2n_ready, i + 1)
                sp.dma_start(h2_rows[bass.ts(i, P), :] if m == P else h2_rows[SEQ:T, :],
                             xn2[0:m, :]).then_inc(h2_stored, 16)

            with sp.Fori(0, LAST - 1) as i:
                store_h2(i)
            sp.wait_ge(p_copied, LAST)
            sp.dma_start(pool_p[0, 0], p[P - STATE:P, :]).then_inc(p7_stored, 16)
            store_h2(LAST - 1)
            sp.wait_ge(p_copied, NT)
            for b in range(DEC):
                sp.dma_start(pool_s[0, b, STATE - DSEQ:STATE, :],
                             p[b * DSEQ:(b + 1) * DSEQ, :]).then_inc(outs, 16)
            sp.wait_ge(v_ready, NT)
            sp.dma_start(v_s[0].rearrange("b s c -> (b s) c"), v[0:NS, :]).then_inc(outs, 16)
            store_h2(LAST, NS)
            sp.wait_ge(outs, 16 * (DEC + 1))

            def chunk_src(e, c):
                half = c % 2
                if c < 4:
                    w = (exp_w1, exp_w3)[c // 2]
                    return w[0, e].rearrange("(p k) n -> p (k n)", k=KD)[:, half * CHW:(half + 1) * CHW]
                return exp_w2[0, e, half * 2 * P:(half + 1) * 2 * P, :].rearrange("(k p) n -> p k n", p=P)

            def chunk_dst(n, c):
                return chunk[n] if c < 4 else chunk[n].rearrange("p (k n) -> p k n", k=2)

            def load_weights(h):
                for n in range(2 * CH):
                    s, c = n // CH, n % CH
                    if isinstance(h, int):
                        sp.wait_ge(proj_p if n < CH else out_b, NT)
                        if n >= 2:
                            sp.wait_ge(chunk_in[n - 2], 16)
                    else:
                        before = sp.to_reg(CH * (2 * h + s - 2) + c + 1)
                        landed = sp.to_reg(16 * h + (16 if n >= 2 else 0))
                        sp.wait_ge(out_b, NT)
                        sp.wait_ge(used, before)
                        sp.wait_ge(chunk_in[n - 2], landed)
                    sp.dma_start(chunk_dst(n, c), chunk_src(2 * h + s, c)).then_inc(chunk_in[n], 16)
                    if isinstance(h, int) and n == CH - 1:
                        tv = slot_table.rearrange("(e r) c -> r e c", r=REG)
                        sp.wait_ge(table_stored, 16 * 2 * NT)
                        for part, es in enumerate((slice(0, 2), slice(2, NE))):
                            sp.dma_start(tabs[:, es, :], tv[0:P, es, :]).then_inc(tabs_in[part], 16)

            load_weights(0)
            with sp.Fori(1, NE // 2) as h:
                load_weights(h)

            sp.wait_ge(plan_ready, 1)
            over = sp.value_load(plan[0:1, 2 * MAXO:2 * MAXO + 1], min_val=0, max_val=MAXO)
            with sp.If(over > 0):
                with sp.Fori(0, over) as g:
                    e = sp.value_load(plan[0:1, bass.ds(g, 1)], min_val=0, max_val=NE - 1)
                    sp.wait_ge(ov_free, g + 1)
                    for c in range(CH):
                        sp.dma_start(chunk_dst(c, c), chunk_src(e, c)).then_inc(ov_w, 16)

            for s in range(2):
                sp.wait_ge(rows_out[s], 16 * (NE // 2))
            sp.wait_ge(state_moved, 16)
            sp.wait_ge(ov_free, over + 1)
            for j in range(NT):
                m = P if j < LAST else NS
                src = pair_rows[2 * P * j:2 * P * j + 2 * m, :]
                sp.dma_start(ypair[j][0:m, :], src.rearrange("(t c) d -> t (c d)", c=2)).then_inc(pair_in[j], 16)
            for j in range(NT):
                sp.wait_ge(y_out, j + 1)
                dst, m = (y_prompt[0, j * P:(j + 1) * P, :], P) if j < LAST else \
                    (y_sample.rearrange("b s d -> (b s) d"), NS)
                sp.dma_start(dst, ypair[j][0:m, 0:D]).then_inc(y_stored, 16)
            sp.wait_ge(y_stored, 16 * NT)

        @block.gpsimd
        def _(pool):
            pool.memset(wst_s[:, :, :], 0.0).then_inc(zeroed, 1)
            pool.memset(xg[0][:, :].bitcast(I32), NOWHERE).then_inc(filled, 1)
            pool.memset(xg[1][:, :], 0.0).then_inc(filled, 1)
            pool.memset(ones[:, :], 1.0).then_inc(filled, 1)
            pool.memset(rd[:, :, :], 0.0).then_inc(filled, 1)
            pool.memset(vd[:, :], 0.0).then_inc(filled, 1)
            pool.wait_ge(in_small, 16 * len(small))
            for w, m in ((wst, P), (wst_s, NS)):
                if w is wst_s:
                    pool.wait_ge(in_late, 16 * len(late))
                pool.affine_select(out=w[0:m, :, :], in_=w[0:m, :, :], compare_op=ALU.is_ge, fill=0.0,
                                   base=0, pattern=[[0, HEADS], [1, m]], channel_multiplier=-1)\
                    .then_inc(wst_masked, 1)

            pool.wait_ge(in_filler, 16)
            for j in range(NT):
                m = P if j < LAST else NS
                pool.wait_ge(dest_ready, j + 1)
                for c in range(2):
                    pool.indirect_dma_start(
                        slot_table, bass.IndirectOffsetOnAxis(ap=dest[0:m, j, c:c + 1], axis=0),
                        ids[0:m, j, c, :], None, bounds_check=NE * REG - 1, oob_is_err=False)\
                        .then_inc(table_stored, 16)
            pool.memset(xg[0][:, :], 0.0).then_inc(filled, 1)
            pool.wait_ge(filled, 6)
            pool.wait_ge(h2_stored, 16 * NT)
            last_token, last_pair = pool.to_reg(T - 1), pool.to_reg(2 * T - 1)

            def gather(dst, idx, done):
                pool.indirect_dma_start(
                    dst, None, h2_rows, bass.IndirectOffsetOnAxis(ap=idx.bitcast(U32), axis=0),
                    bounds_check=last_token, oob_is_err=False).then_inc(done, 16)

            def scatter(src, idx, done):
                pool.indirect_dma_start(
                    pair_rows, bass.IndirectOffsetOnAxis(ap=idx.bitcast(U32), axis=0), src, None,
                    bounds_check=last_pair, oob_is_err=False).then_inc(done, 16)

            def fetch(b, s):
                pool.tensor_copy(gidx[s][:, :], tabs[:, b, 0:1]).then_inc(gidx_ready, 1)
                count = pool.to_reg(b + 1) if not isinstance(b, int) else b + 1
                pool.wait_ge(filled, 6)
                pool.wait_ge(gidx_ready, count)
                gather(xg[s][:, :], gidx[s][:, :], rows_in[s])

            def block_pair(h, last=False):
                for s in range(2):
                    b = 2 * h + s
                    if not last:
                        pool.wait_ge(xgT_done, b + 1)
                        pool.wait_ge(rows_in[s], 16 * h + 16)
                        fetch(b + 2, s)
                    if not_first(h):
                        pool.wait_ge(rows_out[s], 16 * h)
                    pool.tensor_copy(sidx[s][:, :], tabs[:, b, 1:2]).then_inc(sidx_ready, 1)
                    count = b + 1 if isinstance(b, int) else pool.to_reg(b + 1)
                    pool.wait_ge(table_stored, 16 * 2 * NT)
                    pool.wait_ge(sidx_ready, count)
                    pool.wait_ge(y_ready, count)
                    scatter(ys[s][:, :], sidx[s][:, :], rows_out[s])

            pool.wait_ge(tabs_in[0], 16)
            for s in range(2):
                fetch(s, s)
            pool.wait_ge(tabs_in[1], 16)
            block_pair(0)
            with pool.Fori(1, NE // 2 - 1) as h:
                block_pair(h)
            block_pair(NE // 2 - 1, last=True)

            for s in range(2):
                pool.wait_ge(rows_out[s], 16 * (NE // 2))
            pool.wait_ge(plan_ready, 1)
            over = pool.value_load(plan[0:1, 2 * MAXO:2 * MAXO + 1], min_val=0, max_val=MAXO)
            pool.memset(oidx[:, :], 0).then_inc(ov_free, 1)
            with pool.If(over > 0):
                with pool.Fori(0, over) as g:
                    row = pool.value_load(plan[0:1, bass.ds(g + MAXO, 1)], min_val=0, max_val=NE * REG - P)
                    turn = pool.to_reg(16 * g + 16)
                    pool.wait_ge(ov_free, g + 1)
                    pool.dma_start(oidx[:, :], slot_table[bass.ds(row, P), :]).then_inc(ov_idx, 16)
                    pool.wait_ge(filled, 6)
                    pool.wait_ge(ov_idx, turn)
                    gather(xg[0][:, :], oidx[:, 0:1], ov_rows)
                    count = pool.to_reg(g + 1)
                    pool.wait_ge(filled, 6)
                    pool.wait_ge(ov_y, count)
                    scatter(ys[0][:, :], oidx[:, 1:2], ov_out)
                    pool.wait_ge(filled, 6)
                    pool.wait_ge(ov_rows, turn)
                    pool.wait_ge(ov_out, turn)
                    pool.memset(gidx[0][:, :], 0).then_inc(ov_free, 1)

        @block.scalar
        def _(act):
            def square1(i, m, x):
                reached(act, rs1, i)
                act.activation(junk[0:m, :], x, ACT.Square, accum_out=ss1[0:m, 0:1]).then_inc(sq1, 1)

            def step(i, cur, prev, pprev, nxt):
                if prev:
                    m = m_of(prev)
                    act.wait_ge(x2_ready, i)
                    reached(act, rs2, i - 1)
                    reached(act, x2T_done, i - 1)
                    reached(act, h2_stored, 16 * (i - 1))
                    act.activation(xn2[0:m, :], xres[0:m, i - 1, :], ACT.Square,
                                   accum_out=ss2[0:m, 0:1]).then_inc(sq2, 1)
                if nxt:
                    m = m_of(nxt)
                    if isinstance(i, int) and i < 2:
                        act.wait_ge((in_x1, in_x)[i], (16, 32)[i])
                    square1(i + 1, m, xres[0:m, i + 1, :])
                if cur:
                    m = m_of(cur)
                    act.wait_ge(proj_v, i + 1)
                    reached(act, v_ready, i)
                    act.activation(vg[0:m, :], ps[0:m, 2, :], ACT.Gelu).then_inc(v_gelu, 1)
                    act.wait_ge(proj_u, i + 1)
                    reached(act, ya_ready, i)
                    act.activation(u[0:m, :], ps[0:m, 3, :], ACT.Gelu).then_inc(u_gelu, 1)
                    act.wait_ge(proj_p, i + 1)
                    reached(act, ptail_ready, i)
                    if cur == "sample":
                        act.wait_ge(p7_stored, 16)
                    act.activation(p[0:m, :], ps[0:m, 4, :], ACT.Copy).then_inc(p_copied, 1)
                    act.wait_ge(pooled, i + 1)
                    act.activation(poolT[:, :, 0:m],
                                   ps[:, 6, :].rearrange("p (g n) -> p g n", n=P)[:, :, 0:m],
                                   ACT.Copy).then_inc(poolT_ready, 1)
                    act.wait_ge(yaT_done, i + 1)
                    act.activation(yT[:, 0:HEADS, 0:m],
                                   ps[:, 5, :].rearrange("p (k n) -> p k n", n=P)[:, :, 0:m],
                                   ACT.Copy).then_inc(yaT_ready, 1)

            act.wait_ge(in_x0, 16)
            square1(0, P, xres[:, 0, :])
            pipeline(act, step)

            act.wait_ge(dest_ready, NT)
            act.activation(rd[:, :, :], rd[:, :, :], ACT.Exp).then_inc(gate_exp, 1)
            act.activation(vd[:, :], vd[:, :], ACT.Exp).then_inc(gate_exp, 1)

            def block_pair(h):
                for s in range(2):
                    b = 2 * h + s
                    act.wait_ge(used, CH * b + 2)
                    act.activation(s1[:, :], ps[:, 2, :], ACT.Silu).then_inc(silu_done, 1)
                    act.wait_ge(hhaT_done, b + 1)
                    act.activation(hhT[:, 0:2, :], ps[:, 7, 0:2 * P].rearrange("p (k n) -> p k n", n=P),
                                   ACT.Copy).then_inc(hhaT_ready, 1)
                    act.wait_ge(used, CH * b + CH)
                    if not_first(h):
                        act.wait_ge(rows_out[s], 16 * h)
                    act.activation(ys[s][:, :], ps[:, 5:7, :].rearrange("p a n -> p (a n)"), ACT.Copy)\
                        .then_inc(y_ready, 1)

            block_pair(0)
            with act.Fori(1, NE // 2) as h:
                block_pair(h)

            over = act.value_load(plan[0:1, 2 * MAXO:2 * MAXO + 1], min_val=0, max_val=MAXO)
            with act.If(over > 0):
                with act.Fori(0, over) as g:
                    act.wait_ge(ov_up, 2 * g + 1)
                    act.activation(s1[:, :], ps[:, 2, :], ACT.Silu).then_inc(ov_silu, 1)
                    act.wait_ge(ov_down, g + 1)
                    act.activation(ys[0][:, :], ps[:, 5:7, :].rearrange("p a n -> p (a n)"), ACT.Copy)\
                        .then_inc(ov_y, 1)

            for j in range(NT):
                m = P if j < LAST else NS
                act.wait_ge(x3_ready, j + 1)
                reached(act, sq3, j)
                act.activation(junk[0:m, :], xres[0:m, j, :], ACT.Square,
                               accum_out=ssf[0:m, 0, j:j + 1]).then_inc(sq3, 1)

        @block.vector
        def _(dve):
            def run(chain, step, turn, done):
                for n, op in enumerate(chain[:-1]):
                    op().then_inc(step, 1)
                    dve.wait_ge(step, (len(chain) - 1) * turn + n + 1)
                chain[-1]().then_inc(done, 1)

            def rstd(w, src, scale, step, turn, done, several=False):
                a, y, t = w[:, 2:3], w[:, 1:2], w[:, 3:4]
                chain = [lambda: dve.tensor_scalar(a, src, scale, EPS, ALU.mult, ALU.add),
                         lambda: dve.tensor_scalar(t.bitcast(I32), a.bitcast(I32), 1, None,
                                                   ALU.arith_shift_right),
                         lambda: dve.tensor_scalar(y.bitcast(I32), t.bitcast(I32), -1.0, float(0x5f3759df),
                                                   ALU.mult, ALU.add)]
                for _ in range(3):
                    chain += [lambda: dve.tensor_tensor(t, y, y, ALU.mult),
                              lambda: dve.tensor_tensor(t, t, a, ALU.mult)] if several else \
                             [lambda: dve.scalar_tensor_tensor(t, y, a, y, ALU.mult, ALU.mult)]
                    chain += [lambda: dve.tensor_scalar(t, t, -0.5, 1.5, ALU.mult, ALU.add),
                              lambda: dve.tensor_tensor(y, y, t, ALU.mult)]
                run(chain, step, turn, done)

            def norm1(i, m, x):
                dve.wait_ge(sq1, i + 1)
                rstd(ss1[0:m, :], ss1[0:m, 0:1], 1.0 / D, rs1_step, i, rs1)
                dve.wait_ge(rs1, i + 1)
                reached(dve, xT_done, i)
                dve.tensor_scalar(xn[0:m, :], x, ss1[0:m, 1:2], None, ALU.mult).then_inc(xn_ready, 1)

            def take_hT(i, m):
                dve.wait_ge(xT_done, i + 1)
                reached(dve, proj_p, i)
                dve.tensor_tensor(hT[:, :, 0:m], wide[:, :, 0:m],
                                  g1t[:, :].unsqueeze(2).to_broadcast([P, KD, m]), ALU.mult)\
                    .then_inc(hT_ready, 1)

            def choose(i, m):
                l1, l2 = logits[0:m, 0:NG], logits[0:m, NG:NR]
                rev4, rev32 = crow[0:m, 0:NG], crow[0:m, NG:NR]
                r, a, e = rv[0:m, :], ra[0:m, :], rm[0:m, :]
                groups = lambda x: x.rearrange("p (g e) -> p g e", e=EPG)
                spread = lambda x: x.unsqueeze(2).to_broadcast([m, NG, EPG])
                chain = [lambda: dve.tensor_tensor(logits[0:m, :], ps[0:m, 7, 0:NR], rb[0:m, :], ALU.add),
                         lambda: dve.tensor_reduce(r[:, 0:1], l1, AX, ALU.max),
                         lambda: dve.tensor_scalar(rd[0:m, i, :], l1, r[:, 0:1], None, ALU.subtract),
                         lambda: dve.scalar_tensor_tensor(a[:, 0:NG], l1, r[:, 0:1], rev4, ALU.is_equal, ALU.mult),
                         lambda: dve.tensor_reduce(r[:, 1:2], a[:, 0:NG], AX, ALU.max),
                         lambda: dve.tensor_scalar(a[:, NG:2 * NG], rev4, r[:, 1:2], None, ALU.is_equal),
                         lambda: dve.tensor_scalar(a[:, 2 * NG:], a[:, NG:2 * NG], 1.0, BIG, ALU.subtract, ALU.mult),
                         lambda: dve.tensor_tensor(groups(e), groups(l2), spread(a[:, NG:2 * NG]), ALU.mult),
                         lambda: dve.tensor_tensor(groups(e), groups(e), spread(a[:, 2 * NG:]), ALU.add)]
                for c in range(2):
                    v, w, o = r[:, 2 + c:3 + c], r[:, 4:5], oh[c][0:m, :]
                    chain += [lambda v=v: dve.tensor_reduce(v, e, AX, ALU.max),
                              lambda v=v, o=o: dve.scalar_tensor_tensor(o, e, v, rev32, ALU.is_equal, ALU.mult),
                              lambda o=o, w=w: dve.tensor_reduce(w, o, AX, ALU.max),
                              lambda o=o, w=w: dve.tensor_scalar(o, rev32, w, None, ALU.is_equal)]
                    if c == 0:
                        chain.append(lambda o=o: dve.scalar_tensor_tensor(e, o, -2.0 * BIG, e, ALU.mult, ALU.add))
                chain += [lambda: dve.tensor_tensor(vd[0:m, bass.ds(i, 1)], r[:, 3:4], r[:, 2:3], ALU.subtract),
                          lambda: dve.tensor_tensor(mk[0:m, :], oh[0][0:m, :], oh[1][0:m, :], ALU.add)]
                chain[0]().then_inc(logits_ready, 1)
                dve.wait_ge(logits_ready, i + 1)
                run(chain[1:], r1_step, i, mk_ready)

            def place(i, m):
                dve.wait_ge(rank_done, i + 1)
                dve.tensor_tensor(rs[0:m, :], ps[0:m, 5, 0:NE], base[0:m, :], ALU.add).then_inc(r2_step, 1)
                dve.wait_ge(r2_step, 4 * i + 1)
                dve.tensor_tensor(base[:, :], base[:, :], ps[:, 5, NE:2 * NE], ALU.add).then_inc(rank_taken, 1)
                for c in range(2):
                    dve.scalar_tensor_tensor(oh[c][0:m, :], oh[c][0:m, :], 1.0, rs[0:m, :], ALU.mult, ALU.mult)\
                        .then_inc(r2_step, 1)
                    dve.wait_ge(r2_step, 4 * i + 2 + c)
                for c in range(2):
                    last = dve.tensor_reduce(destf[0:m, c:c + 1], oh[c][0:m, :], AX, ALU.add)
                last.then_inc(r2_step, 1)
                dve.wait_ge(r2_step, 4 * i + 4)
                dve.tensor_copy(dest[0:m, i, :], destf[0:m, :]).then_inc(dest_ready, 1)

            def step(i, cur, prev, pprev, nxt):
                if isinstance(i, int) and i == 1:
                    dve.wait_ge(in_late, 16 * len(late))
                if prev:
                    m = m_of(prev)
                    dve.wait_ge(out_a, i)
                    dve.tensor_tensor(xres[0:m, i - 1, 0:512], xres[0:m, i - 1, 0:512], ps[0:m, 6, :],
                                      ALU.add).then_inc(x2a_ready, 1)
                    dve.wait_ge(out_b, i)
                    dve.tensor_tensor(xres[0:m, i - 1, 512:D], xres[0:m, i - 1, 512:D], ps[0:m, 7, :],
                                      ALU.add).then_inc(x2_ready, 1)
                if pprev:
                    place(i - 2, m_of(pprev))
                if prev:
                    dve.wait_ge(sq2, i)
                    rstd(ss2[0:m, :], ss2[0:m, 0:1], 1.0 / D, rs2_step, i - 1, rs2)
                    dve.wait_ge(rs2, i)
                    reached(dve, x2T_done, i - 1)
                    reached(dve, h2_stored, 16 * (i - 1))
                    dve.tensor_scalar(xn2[0:m, :], xres[0:m, i - 1, :], ss2[0:m, 1:2], None, ALU.mult)\
                        .then_inc(x2n_ready, 1)
                if nxt:
                    norm1(i + 1, m_of(nxt), xres[0:m_of(nxt), i + 1, :])
                if cur:
                    m = m_of(cur)
                    dve.wait_ge(v_gelu, i + 1)
                    dve.bn_stats(lnst[0:m, 0:6], vg[0:m, :]).then_inc(ln_step, 1)
                    stats = dve.to_reg(4 * i + 1)
                    dve.wait_ge(in_small, 16 * len(small))
                    dve.wait_ge(ln_step, stats)
                    dve.bn_aggr(lnst[0:m, 6:8], lnst[0:m, 0:6]).then_inc(ln_step, 1)
                    dve.wait_ge(ln_step, 4 * i + 2)
                    rstd(lnst[0:m, 8:12], lnst[0:m, 7:8], 1.0, ln_rs_step, i, ln_rs)
                    dve.wait_ge(ln_rs, i + 1)
                    reached(dve, z_done, i)
                    dve.tensor_scalar(v[0:m, :], vg[0:m, :], lnst[0:m, 6:7], lnst[0:m, 9:10],
                                      ALU.subtract, ALU.mult).then_inc(ln_step, 1)
                    dve.wait_ge(ln_step, 4 * i + 3)
                    dve.tensor_tensor(v[0:m, :], v[0:m, :], ag[0:m, :], ALU.mult).then_inc(ln_step, 1)
                    dve.wait_ge(ln_step, 4 * i + 4)
                    dve.tensor_tensor(v[0:m, :], v[0:m, :], ab[0:m, :], ALU.add).then_inc(v_ready, 1)
                if cur:
                    m = m_of(cur)
                    dve.wait_ge(z_done, i + 1)
                    dve.wait_ge(u_gelu, i + 1)
                    reached(dve, yaT_done, i)
                    bias = bst_s if cur == "sample" else bst
                    for h in range(HEADS):
                        c = slice(h * P, (h + 1) * P)
                        last = dve.scalar_tensor_tensor(ya[0:m, c], ps[0:m, 5, c], bias[0:m, h:h + 1],
                                                        u[0:m, c], ALU.add, ALU.mult)
                    last.then_inc(ya_ready, 1)
                    dve.wait_ge(pooled, i + 1)
                    dve.tensor_copy(ptail[0:m, :], p[0:m, :]).then_inc(ptail_ready, 1)
                if nxt:
                    take_hT(i + 1, m_of(nxt))
                if cur:
                    m = m_of(cur)
                    dve.wait_ge(yb_done, i + 1)
                    reached(dve, out_b, i)
                    dve.tensor_tensor(yT[:, HEADS:KD, 0:m],
                                      ps[:, 6, :].rearrange("p (g n) -> p g n", n=P)[:, :, 0:m],
                                      bsc[:, :].unsqueeze(2).to_broadcast([P, GROUPS, m]), ALU.mult)\
                        .then_inc(ybT_ready, 1)
                if prev:
                    m = m_of(prev)
                    dve.wait_ge(x2T_done, i)
                    reached(dve, logit_done, i - 1)
                    dve.tensor_tensor(h2T[:, :, 0:m], wide[:, :, 0:m],
                                      g2t[:, :].unsqueeze(2).to_broadcast([P, KD, m]), ALU.mult)\
                        .then_inc(h2T_ready, 1)
                    dve.wait_ge(logit_done, i)
                    choose(i - 1, m)

            dve.wait_ge(in_x0, 16)
            norm1(0, P, xres[:, 0, :])
            dve.wait_ge(in_first, 32)
            take_hT(0, P)
            dve.wait_ge(filled, 5)
            pipeline(dve, step)

            dve.wait_ge(gate_exp, 2)
            run([lambda: dve.tensor_reduce(gate[0][:, :], rd[:, :, :], AX, ALU.add),
                 lambda: dve.scalar_tensor_tensor(gate[0][:, :], vd[:, :], 1.0, gate[0][:, :], ALU.add, ALU.mult),
                 lambda: dve.reciprocal(gate[0][:, :], gate[0][:, :]),
                 lambda: dve.tensor_tensor(gate[1][:, :], gate[0][:, :], vd[:, :], ALU.mult),
                 ], gate_step, 0, gate_step)
            own, end, one = blk[:, 0, :], blk[:, 1, :], blk[:, 2, :]
            numbers, thresholds = crow[0:1, NR:NR + MAXO], crow[0:1, NR + MAXO:]
            over_k = junk[0:1, 512:512 + NE * OVER].rearrange("p (e k) -> p e k", k=OVER)
            by_n = lambda x: x.unsqueeze(1).to_broadcast([1, MAXO, NE])
            run([lambda: dve.tensor_tensor(blk[:, 3, :], base[0:1, :], base0[0:1, :], ALU.subtract),
                 lambda: dve.memset(one, 1.0),
                 lambda: dve.tensor_tensor(over_k, blk[:, 3, :].unsqueeze(2).to_broadcast([1, NE, OVER]),
                                           thresholds.unsqueeze(1).to_broadcast([1, NE, OVER]), ALU.is_gt),
                 lambda: dve.tensor_reduce(own, over_k, AX, ALU.add),
                 lambda: dve.tensor_tensor_scan(end, one, own, 0.0, ALU.mult, ALU.add),
                 lambda: dve.tensor_tensor(cmp, by_n(end), numbers.unsqueeze(2).to_broadcast([1, MAXO, NE]),
                                           ALU.is_le),
                 lambda: dve.tensor_reduce(planf[:, 0:MAXO], cmp, AX, ALU.add),
                 lambda: dve.tensor_scalar(planf[:, 0:MAXO], planf[:, 0:MAXO], float(NE - 1), None, ALU.min),
                 lambda: dve.tensor_tensor(cmp, cmp, by_n(end), ALU.mult),
                 lambda: dve.tensor_reduce(planf[:, MAXO:2 * MAXO], cmp, AX, ALU.max),
                 lambda: dve.tensor_tensor(planf[:, MAXO:2 * MAXO], numbers, planf[:, MAXO:2 * MAXO], ALU.subtract),
                 lambda: dve.tensor_scalar(planf[:, MAXO:2 * MAXO], planf[:, MAXO:2 * MAXO], 1.0, float(P),
                                           ALU.add, ALU.mult),
                 lambda: dve.scalar_tensor_tensor(planf[:, MAXO:2 * MAXO], planf[:, 0:MAXO], float(REG),
                                                  planf[:, MAXO:2 * MAXO], ALU.mult, ALU.add),
                 lambda: dve.tensor_scalar(planf[:, MAXO:2 * MAXO], planf[:, MAXO:2 * MAXO],
                                           float(NE * REG - P), None, ALU.min),
                 lambda: dve.tensor_copy(planf[:, 2 * MAXO:], end[:, NE - 1:NE]),
                 lambda: dve.tensor_copy(plan[:, :], planf[:, :])], plan_step, 0, plan_ready)

            def take_xgT(b):
                dve.wait_ge(xgT_done, b + 1)
                dve.tensor_tensor(xT[:, :, :], wide, g2t[:, :].unsqueeze(2).to_broadcast([P, KD, P]),
                                  ALU.mult).then_inc(xgT_ready, 1)

            def block_pair(h, last=False):
                for s in range(2):
                    b = 2 * h + s
                    dve.wait_ge(silu_done, b + 1)
                    dve.wait_ge(up3a, b + 1)
                    dve.tensor_tensor(hh[:, 0:256], s1[:, 0:256], ps[:, 3, 0:256], ALU.mult).then_inc(hha_ready, 1)
                    dve.wait_ge(used, CH * b + 4)
                    dve.tensor_tensor(hh[:, 256:512], s1[:, 256:512], ps[:, 4, 0:256], ALU.mult)\
                        .then_inc(hhb_ready, 1)
                    if not (last and s):
                        take_xgT(b + 1)
                    dve.wait_ge(hhbT_done, b + 1)
                    dve.tensor_copy(hhT[:, 2:4, :], ps[:, 2, 0:2 * P].rearrange("p (k n) -> p k n", n=P))\
                        .then_inc(hhbT_ready, 1)

            take_xgT(0)
            block_pair(0)
            with dve.Fori(1, NE // 2 - 1) as h:
                block_pair(h)
            block_pair(NE // 2 - 1, last=True)

            dve.wait_ge(plan_ready, 1)
            over = dve.value_load(plan[0:1, 2 * MAXO:2 * MAXO + 1], min_val=0, max_val=MAXO)
            with dve.If(over > 0):
                with dve.Fori(0, over) as g:
                    dve.wait_ge(ov_xT, g + 1)
                    dve.tensor_tensor(xT[:, :, :], wide, g2t[:, :].unsqueeze(2).to_broadcast([P, KD, P]),
                                      ALU.mult).then_inc(ov_x, 1)
                    dve.wait_ge(ov_silu, g + 1)
                    dve.wait_ge(ov_up, 2 * g + 2)
                    dve.tensor_tensor(hh[:, :], s1[:, :], ps[:, 3, :], ALU.mult).then_inc(ov_hh, 1)
                    dve.wait_ge(ov_hT, g + 1)
                    dve.tensor_copy(hhT[:, :, :], ps[:, 4, :].rearrange("p (k n) -> p k n", n=P))\
                        .then_inc(ov_h, 1)

            def add_pair(j):
                m = P if j < LAST else NS
                yp, x = ypair[j], xres[0:m, j, :]
                dve.wait_ge(pair_in[j], 16)
                dve.scalar_tensor_tensor(x, yp[0:m, 0:D], gate[0][0:m, j:j + 1], x, ALU.mult, ALU.add)\
                    .then_inc(pair_sum, 1)
                dve.wait_ge(pair_sum, j + 1)
                dve.scalar_tensor_tensor(x, yp[0:m, D:2 * D], gate[1][0:m, j:j + 1], x, ALU.mult, ALU.add)\
                    .then_inc(x3_ready, 1)

            def norm_tiles(turn, tiles):
                dve.wait_ge(sq3, tiles[-1] + 1)
                w = ssf[:, :, tiles[0]:tiles[-1] + 1]
                rstd(w, w[:, 0:1], 1.0 / D, rs3_step, turn, rs3, several=True)
                dve.wait_ge(rs3, turn + 1)
                for j in tiles:
                    m = P if j < LAST else NS
                    dve.scalar_tensor_tensor(ypair[j][0:m, 0:D], xres[0:m, j, :], ssf[0:m, 1, j:j + 1],
                                             gf[0:m, :], ALU.mult, ALU.mult).then_inc(y_out, 1)

            dve.memset(ssf[:, :, :], 1.0).then_inc(ssf_set, 1)
            dve.wait_ge(ssf_set, 1)
            dve.wait_ge(gate_step, 4)
            groups = [(0, 1), (2, 3), (4, 5), (6, 7), (8,)]
            for turn, tiles in enumerate(groups):
                for j in tiles:
                    add_pair(j)
                if turn:
                    norm_tiles(turn - 1, groups[turn - 1])
            norm_tiles(len(groups) - 1, groups[-1])

        @block.tensor
        def _(pe):
            def turn(x, m, done, k=KD, bank=0):
                xs = x[0:m, :].rearrange("t (p k) -> t k p", k=k)
                for c in range(k):
                    last = pe.transpose(ps[:, bank + c // 4, (c % 4) * P:(c % 4) * P + m], xs[:, c, :],
                                        ident[0:m, 0:m])
                last.then_inc(done, 1)

            def step(i, cur, prev, pprev, nxt):
                if isinstance(i, int) and i == 1:
                    pe.wait_ge(in_late, 16 * len(late))
                    pe.wait_ge(wst_masked, 2)
                if pprev:
                    m = m_of(pprev)
                    pe.wait_ge(mk_ready, i - 1)
                    pe.matmul(ps[0:m, 5, 0:NE], tri[0:m, 0:m], mk[0:m, :], start=True, stop=True)
                    pe.matmul(ps[:, 5, NE:2 * NE], ones[0:m, :], mk[0:m, :], start=True, stop=True)\
                        .then_inc(rank_done, 1)
                if cur:
                    m = m_of(cur)
                    pe.wait_ge(hT_ready, i + 1)
                    for bank, part, free, done in ((2, 1, v_gelu, proj_v), (3, 0, u_gelu, proj_u),
                                                   (4, 2, p_copied, proj_p)):
                        reached(pe, free, i)
                        for k in range(KD):
                            if isinstance(i, int) and i == 0 and bank == 2 and k % 2 == 0:
                                pe.wait_ge(in_win[k // 2], 16)
                            last = pe.matmul(ps[0:m, bank, :], hT[:, k, 0:m], win[:, k, part * AW:(part + 1) * AW],
                                             start=(k == 0), stop=(k == KD - 1))
                        last.then_inc(done, 1)
                    w = wst_s if cur == "sample" else wst
                    pe.wait_ge(v_ready, i + 1)
                    if pprev:
                        pe.wait_ge(rank_taken, i - 1)
                    if isinstance(i, int) and i == 0:
                        pe.wait_ge(in_small, 16 * len(small))
                        pe.wait_ge(wst_masked, 1)
                    for h in range(HEADS):
                        last = pe.matmul(ps[0:m, 5, h * P:(h + 1) * P], w[0:m, h, 0:m],
                                         v[0:m, h * P:(h + 1) * P], start=True, stop=True)
                    last.then_inc(z_done, 1)
                    pe.wait_ge(p_copied, i + 1)
                    reached(pe, ptail_ready, i)
                    reached(pe, x2a_ready, i)
                    parts = {"first": [(p, band_first, P)], "mid": [(p, band, P), (ptail, band_prev, P)],
                             "sample": [(p, band_s, NS), (state, band_state, DEC * STATE)]}[cur]
                    for g in range(GROUPS):
                        for n, (src, bnd, kk) in enumerate(parts):
                            last = pe.matmul(ps[:, 6, g * P:g * P + m], src[0:kk, g * P:(g + 1) * P],
                                             bnd[0:kk, g, 0:m], start=(n == 0), stop=(n == len(parts) - 1))
                    last.then_inc(pooled, 1)
                if nxt:
                    pe.wait_ge(xn_ready, i + 2)
                    reached(pe, h2T_ready, i - 1)
                    turn(xn, m_of(nxt), xT_done)
                if cur:
                    m = m_of(cur)
                    pe.wait_ge(ya_ready, i + 1)
                    turn(ya, m, yaT_done, HEADS, 5)
                    pe.wait_ge(poolT_ready, i + 1)
                    for g in range(GROUPS):
                        last = pe.matmul(ps[:, 6, g * P:g * P + m], bw[:, g, :], poolT[:, g, 0:m],
                                         start=True, stop=True)
                    last.then_inc(yb_done, 1)
                if prev:
                    pe.wait_ge(x2n_ready, i)
                    if nxt:
                        pe.wait_ge(hT_ready, i + 2)
                    turn(xn2, m_of(prev), x2T_done)
                    m = m_of(prev)
                    pe.wait_ge(h2T_ready, i)
                    for k in range(KD):
                        last = pe.matmul(ps[0:m, 7, 0:NR], h2T[:, k, 0:m], rw[:, k, :],
                                         start=(k == 0), stop=(k == KD - 1))
                    last.then_inc(logit_done, 1)
                if cur:
                    m = m_of(cur)
                    if isinstance(i, int) and i == 0:
                        pe.wait_ge(in_wout, 32)
                    pe.wait_ge(yaT_ready, i + 1)
                    pe.wait_ge(ybT_ready, i + 1)
                    for half, done in ((0, out_a), (1, out_b)):
                        if half:
                            reached(pe, logits_ready, i)
                        for k in range(KD):
                            last = pe.matmul(ps[0:m, 6 + half, :], yT[:, k, 0:m],
                                             wout[:, k, half * 512:(half + 1) * 512],
                                             start=(k == 0), stop=(k == KD - 1))
                        last.then_inc(done, 1)

            pe.wait_ge(in_first, 32)
            pe.wait_ge(xn_ready, 1)
            turn(xn, P, xT_done)
            pipeline(pe, step)

            def turn_hh(half, bank, done):
                for k in range(2):
                    c = (2 * half + k) * P
                    last = pe.transpose(ps[:, bank, k * P:(k + 1) * P], hh[:, c:c + P], ident[:, :])
                last.then_inc(done, 1)

            def up_weights(n):
                return chunk[n].rearrange("p (k n) -> p k n", n=FE)

            def down_weights(n):
                return chunk[n].rearrange("p (k n) -> p k n", n=D)

            def block_pair(h, last_pair=False):
                for s in range(2):
                    b = 2 * h + s
                    pe.wait_ge(xgT_ready, b + 1)
                    if not_first(h, s):
                        pe.wait_ge(hhbT_ready, b)
                    for half in range(2):
                        n = CH * s + half
                        pe.wait_ge(chunk_in[n], 16 * h + 16)
                        for k in range(4):
                            last = pe.matmul(ps[:, 2, :], xT[:, 4 * half + k, :], up_weights(n)[:, k, :],
                                             start=(half + k == 0), stop=(half + k == 4))
                        last.then_inc(used, 1)
                    for cols in range(2):
                        for half in range(2):
                            n = CH * s + 2 + half
                            if cols == 0:
                                pe.wait_ge(chunk_in[n], 16 * h + 16)
                            for k in range(4):
                                last = pe.matmul(ps[:, 3 + cols, 0:256], xT[:, 4 * half + k, :],
                                                 up_weights(n)[:, k, cols * 256:(cols + 1) * 256],
                                                 start=(half + k == 0), stop=(half + k == 4))
                            if cols:
                                last.then_inc(used, 1)
                        if cols == 0:
                            last.then_inc(up3a, 1)
                    pe.wait_ge(hha_ready, b + 1)
                    turn_hh(0, 7, hhaT_done)
                    if not (last_pair and s):
                        pe.wait_ge(rows_in[1 - s], 16 * h + (32 if s else 16))
                        turn(xg[1 - s], P, xgT_done)
                    pe.wait_ge(hhb_ready, b + 1)
                    turn_hh(1, 2, hhbT_done)
                    if not_first(h, s):
                        pe.wait_ge(y_ready, b)
                    pe.wait_ge(hhaT_ready, b + 1)
                    for half in range(2):
                        n = CH * s + 4 + half
                        if half:
                            pe.wait_ge(hhbT_ready, b + 1)
                        pe.wait_ge(chunk_in[n], 16 * h + 16)
                        for k in range(2):
                            for cols in range(2):
                                last = pe.matmul(ps[:, 5 + cols, :], hhT[:, 2 * half + k, :],
                                                 down_weights(n)[:, k, cols * 512:(cols + 1) * 512],
                                                 start=(half + k == 0), stop=(half + k == 2))
                        last.then_inc(used, 1)

            pe.wait_ge(rows_in[0], 16)
            turn(xg[0], P, xgT_done)
            block_pair(0)
            with pe.Fori(1, NE // 2 - 1) as h:
                block_pair(h)
            block_pair(NE // 2 - 1, last_pair=True)

            pe.wait_ge(plan_ready, 1)
            over = pe.value_load(plan[0:1, 2 * MAXO:2 * MAXO + 1], min_val=0, max_val=MAXO)
            with pe.If(over > 0):
                with pe.Fori(0, over) as g:
                    pe.wait_ge(ov_rows, 16 * g + 16)
                    turn(xg[0], P, ov_xT)
                    pe.wait_ge(ov_x, g + 1)
                    pe.wait_ge(ov_w, 16 * CH * g + 16 * CH)
                    for m in range(2):
                        for k in range(KD):
                            last = pe.matmul(ps[:, 2 + m, :], xT[:, k, :], up_weights(2 * m + k // 4)[:, k % 4, :],
                                             start=(k == 0), stop=(k == KD - 1))
                        last.then_inc(ov_up, 1)
                    pe.wait_ge(ov_hh, g + 1)
                    for k in range(KF):
                        last = pe.transpose(ps[:, 4, k * P:(k + 1) * P], hh[:, k * P:(k + 1) * P], ident[:, :])
                    last.then_inc(ov_hT, 1)
                    pe.wait_ge(ov_h, g + 1)
                    for cols in range(2):
                        for k in range(KF):
                            last = pe.matmul(ps[:, 5 + cols, :], hhT[:, k, :],
                                             down_weights(4 + k // 2)[:, k % 2, cols * 512:(cols + 1) * 512],
                                             start=(k == 0), stop=(k == KF - 1))
                    last.then_inc(ov_down, 1)


def constants():
    import numpy as np
    f = np.float32
    s, t = np.arange(P)[:, None], np.arange(P)[None, :]
    w = np.array(WINDOWS)[None, :, None]
    d = (t - s)[:, None, :]
    own = -(d == 0).astype(f)
    c = {"ident": np.eye(P, dtype=f), "tri": (s < t).astype(f)}
    inside = ((d >= 0) & (d < w)).astype(f)
    c["band"] = inside / w.astype(f) + own
    c["band_first"] = inside / np.minimum(t[:, None, :] + 1, w).astype(f) + own
    c["band_prev"] = ((d + P < w).astype(f) / w.astype(f))
    q, r = np.arange(NS) // DSEQ, np.arange(NS) % DSEQ
    same = (q[:, None] == q[None, :])[:, None, :]
    c["band_s"] = (same * c["band"][:NS, :, :NS]).astype(f)
    sq, sr = np.arange(DEC * STATE) // STATE, np.arange(DEC * STATE) % STATE
    ds = (STATE + r[None, :] - sr[:, None])[:, None, :]
    c["band_state"] = ((sq[:, None] == q[None, :])[:, None, :] * (ds < w) / w).astype(f)
    c["row"] = np.concatenate([NG - np.arange(NG), NE - np.arange(NE), np.arange(MAXO),
                               P * (1 + np.arange(OVER))]).astype(f)
    c["base"] = (REG * np.arange(NE)).astype(f)
    ids = np.zeros((P, NT, 2, 2), np.int32)
    tok = np.arange(P)[:, None] + P * np.arange(NT)[None, :]
    for k in range(2):
        ids[:, :, k, 0] = tok
        ids[:, :, k, 1] = 2 * tok + k
    c["ids"] = ids
    return {k: np.ascontiguousarray(v) for k, v in c.items()}


def kernel(**inputs):
    import numpy as np
    import concourse.bacc as bacc
    from concourse.bass_utils import run_bass_kernel_spmd

    a = {k: np.ascontiguousarray(v) for k, v in inputs.items()}
    host = {k: a[k] for k in ("x_prompt", "x_sample", "state_pool", "norm1_g", "w_in", "a_norm_g", "a_norm_b")}
    host["ws_sht"] = np.ascontiguousarray(a["a_ws"][0].transpose(2, 0, 1))
    host["bs_th"] = np.ascontiguousarray(a["a_bs"][0].transpose(1, 0))
    host["bsc_dg"] = np.ascontiguousarray(a["b_scale"][0].reshape(GROUPS, P).T)
    host.update({k: a[k] for k in ("b_w", "w_out", "norm2_g")})
    host["r_w"] = np.concatenate([a["r1_w"][0], a["r2_w"][0].transpose(1, 0, 2).reshape(D, NE)], axis=1)
    host["r_b"] = np.concatenate([a["r1_b"][0], a["r2_b"][0].reshape(NE)])
    host.update({k: a[k] for k in ("exp_w1", "exp_w3", "exp_w2", "normf_g")})
    host.update({f"c_{k}": v for k, v in constants().items()})
    order = ["x_prompt", "x_sample", "state_pool", "norm1_g", "w_in", "a_norm_g", "a_norm_b", "ws_sht", "bs_th",
             "b_w", "bsc_dg", "w_out", "norm2_g", "r_w", "r_b", "exp_w1", "exp_w3", "exp_w2", "normf_g",
             "c_ident", "c_band", "c_band_first", "c_band_prev", "c_band_s", "c_band_state", "c_tri", "c_row", "c_base", "c_ids"]

    nc = bacc.Bacc("TRN2", target_bir_lowering=False, num_devices=1)
    arrays, args = {}, []
    for name in order:
        x = np.ascontiguousarray(host[name])
        arrays[f"in_{name}"] = x
        args.append(nc.dram_tensor(f"in_{name}", x.shape, mybir.dt.from_np(x.dtype), kind="ExternalInput").ap())
    outs = [("y_prompt", (1, SEQ, D)), ("y_sample", (DEC, DSEQ, D)), ("pool_p", (1, 1, STATE, AW)),
            ("pool_s", (1, DEC, STATE, AW)), ("v_s", (1, DEC, DSEQ, AW))]
    for name, shape in outs:
        args.append(nc.dram_tensor(f"out_{name}", shape, F32, kind="ExternalOutput").ap())
    build(nc, *args)
    r = run_bass_kernel_spmd(nc, [arrays], core_ids=[0])
    return tuple(r.results[0][f"out_{name}"] for name, _ in outs)
```
